# Optimizing a Trainium2 kernel written in Bass

```python
import math
import jax, jax.numpy as jnp
from jax import lax
import numpy as np

D_MODEL = 2048
BATCH = 1
SEQ = 512
DEPTH = 1

EXPAND = 2
D_MIX = EXPAND * D_MODEL
W_CONV = D_MIX // 2
W_ATTN = D_MIX - W_CONV
HEAD_DIM = 128
N_HEADS = W_ATTN // HEAD_DIM
CONV_WIDTH = 31
Q_BLOCK = 128
LN_EPS = 1e-5
DN_ALPHA = (2.0 * DEPTH) ** 0.25
DN_BETA = (8.0 * DEPTH) ** -0.25

SPLIT_SIZES = (
    W_CONV,
    W_CONV,
    W_CONV,
    W_ATTN,
    W_ATTN,
    W_ATTN,
    N_HEADS,
    W_ATTN,
)
D_IN = sum(SPLIT_SIZES)

kernel_name = "hybrid_conformer_conv_fox_attn_deepnorm"

def _layer_norm(x, g, b):
    xf = x.astype(jnp.float32)
    mu = jnp.mean(xf, axis=-1, keepdims=True)
    var = jnp.mean(jnp.square(xf - mu), axis=-1, keepdims=True)
    y = (xf - mu) * lax.rsqrt(var + LN_EPS) * g.astype(jnp.float32) + b.astype(jnp.float32)
    return y.astype(x.dtype)

def _split_columns(h):
    offsets = np.cumsum(SPLIT_SIZES)[:-1].tolist()
    return jnp.split(h, offsets, axis=-1)

def _conformer_conv(glu_val, glu_gate, w_dw, b_dw, g_cn, b_cn):
    u = glu_val * jax.nn.sigmoid(glu_gate)
    u_pad = jnp.pad(u, ((0, 0), (CONV_WIDTH - 1, 0), (0, 0)))
    c = lax.conv_general_dilated(
        u_pad, w_dw[:, None, :].astype(u.dtype),
        window_strides=(1,), padding="VALID",
        dimension_numbers=("NWC", "WIO", "NWC"),
        feature_group_count=W_CONV) + b_dw
    c = _layer_norm(c, g_cn, b_cn)
    return jax.nn.silu(c)

def _forgetting_attention(q, k, v, f_logit):
    b, s, _ = q.shape
    to_heads = lambda t: t.reshape(b, s, N_HEADS, HEAD_DIM).transpose(0, 2, 1, 3)
    qh, kh, vh = to_heads(q), to_heads(k), to_heads(v)
    log_f = jax.nn.log_sigmoid(f_logit.astype(jnp.float32)).transpose(0, 2, 1)
    cum = jnp.cumsum(log_f, axis=-1)
    scale = 1.0 / math.sqrt(HEAD_DIM)
    n_blocks = s // Q_BLOCK
    outs = []
    for i in range(n_blocks):
        q0, q1 = i * Q_BLOCK, (i + 1) * Q_BLOCK
        q_blk = qh[:, :, q0:q1]
        k_pre, v_pre = kh[:, :, :q1], vh[:, :, :q1]
        logits = jnp.einsum("bhqd,bhkd->bhqk", q_blk, k_pre).astype(jnp.float32) * scale
        logits = logits + (cum[:, :, q0:q1, None] - cum[:, :, None, :q1])
        q_pos = q0 + jnp.arange(Q_BLOCK)
        k_pos = jnp.arange(q1)
        logits = jnp.where(k_pos[None, :] <= q_pos[:, None], logits, -jnp.inf)
        p = jax.nn.softmax(logits, axis=-1).astype(v_pre.dtype)
        outs.append(jnp.einsum("bhqk,bhkd->bhqd", p, v_pre))
    o = jnp.concatenate(outs, axis=2)
    return o.transpose(0, 2, 1, 3).reshape(b, s, W_ATTN)

def setup_inputs(seed: int = 0) -> dict:
    key = jax.random.key(seed)
    ks = jax.random.split(key, 12)
    x = jax.random.normal(ks[0], (BATCH, SEQ, D_MODEL), jnp.float32)
    w_in = jax.random.normal(ks[1], (D_MODEL, D_IN), jnp.float32) * D_MODEL ** -0.5
    b_small = 0.02 * jax.random.normal(ks[2], (D_IN,), jnp.float32)
    b_forget = 2.0 + 2.0 * jax.random.uniform(ks[3], (N_HEADS,), jnp.float32)
    f_off = sum(SPLIT_SIZES[:6])
    b_in = b_small.at[f_off:f_off + N_HEADS].set(b_forget)
    w_dw = jax.random.normal(ks[4], (CONV_WIDTH, W_CONV), jnp.float32) * CONV_WIDTH ** -0.5
    b_dw = 0.02 * jax.random.normal(ks[5], (W_CONV,), jnp.float32)
    g_conv_norm = 1.0 + 0.05 * jax.random.normal(ks[6], (W_CONV,), jnp.float32)
    b_conv_norm = 0.02 * jax.random.normal(ks[7], (W_CONV,), jnp.float32)
    w_out = jax.random.normal(ks[8], (D_MIX, D_MODEL), jnp.float32) * (D_MIX ** -0.5) * DN_BETA
    b_out = 0.02 * jax.random.normal(ks[9], (D_MODEL,), jnp.float32)
    g_post = 1.0 + 0.05 * jax.random.normal(ks[10], (D_MODEL,), jnp.float32)
    b_post = 0.02 * jax.random.normal(ks[11], (D_MODEL,), jnp.float32)
    return {"x": x, "w_in": w_in, "b_in": b_in, "w_dw": w_dw, "b_dw": b_dw,
            "g_conv_norm": g_conv_norm, "b_conv_norm": b_conv_norm,
            "w_out": w_out, "b_out": b_out, "g_post": g_post, "b_post": b_post}

def reference(x, w_in, b_in, w_dw, b_dw, g_conv_norm, b_conv_norm, w_out, b_out, g_post, b_post):
    h = x
    for _ in range(DEPTH):
        z = jnp.einsum("bsd,de->bse", h, w_in) + b_in
        glu_val, glu_gate, gate_c, q, k, v, f_logit, gate_a = _split_columns(z)
        y_conv = _conformer_conv(glu_val, glu_gate, w_dw, b_dw, g_conv_norm, b_conv_norm)
        y_conv = y_conv * jax.nn.silu(gate_c)
        y_attn = _forgetting_attention(q, k, v, f_logit)
        y_attn = y_attn * jax.nn.silu(gate_a)
        y = jnp.concatenate([y_conv, y_attn], axis=-1)
        sub = jnp.einsum("bse,ed->bsd", y, w_out) + b_out
        h = _layer_norm(DN_ALPHA * h + sub, g_post, b_post)
    return h


_drawn_inputs = setup_inputs


def setup_inputs(seed=0):
    import zlib

    import numpy as np

    out = dict(_drawn_inputs(seed))
    spreads = {}
    factors = {'b_dw': 8.0, 'g_conv_norm': 7.41, 'b_conv_norm': 28.145, 'b_out': 3.336, 'b_post': 2.912}
    for name, (base, spread) in spreads.items():
        noise = np.random.default_rng([zlib.crc32(name.encode()), seed]).standard_normal(out[name].shape)
        drawn = base * np.exp(spread * noise) if base else spread * noise
        out[name] = __import__('jax').numpy.asarray(drawn.astype(out[name].dtype))
    for name, factor in factors.items():
        out[name] = (out[name] * factor).astype(out[name].dtype)
    return out
```

```python
import math
from contextlib import ExitStack

import concourse.bass as bass
from concourse import mybir

F32 = mybir.dt.float32
F32R = mybir.dt.float32r
BF16 = mybir.dt.bfloat16
ACT = mybir.ActivationFunctionType
ALU = mybir.AluOpType
AX = mybir.AxisListType

P = 128
SEQ = 512
D = 2048
KT = D // P
HALF = KT // 2
NT = SEQ // P
HEADS = D // P
TAPS = 31
PAD = TAPS - 1
LN_EPS = 1e-5
ALPHA = 2.0 ** 0.25
SCALE = 1.0 / math.sqrt(P)
MASKED = -1e37

PER_HEAD = 6
T_BODY = 1
T_GATE = T_BODY + PER_HEAD * HEADS
T_OUT = T_GATE + HEADS
OUT_PAIRS = HEADS
N_OUT = 2 * OUT_PAIRS
SLOTS = 4

VAL, GLU, GATE_C, Q, K, V, GATE_A = range(7)
F_COL = 6 * D
BODY_KINDS = (Q, K, V, GATE_A, VAL, GLU)
BODY_TAPS = (7, 7, 7, 6, 5, 0)
B_DW, G_CN, B_CN = range(3)
NOW = {Q: (0, False), K: (1, False), V: (2, False), GATE_A: (3, True), VAL: (4, True), GLU: (5, True)}

PT_N = [SEQ - P * j for j in range(NT)]
PT_AT = [sum(PT_N[:j]) for j in range(NT + 1)]
PR_AT = [P * i * (i + 1) // 2 for i in range(NT + 1)]


def col_of(kind, i):
    return (F_COL + HEADS if kind == GATE_A else kind * D) + P * i


def build(nc, x, w_in, b_in, w_dw, b_dw, g_cn, b_cn, w_out, b_out, g_post, b_post, out, scratch):
    ctx = ExitStack()
    with ctx:
        def sb(name, shape, dt=F32, where=ctx):
            return where.enter_context(nc.sbuf_tensor(name, shape, dt))

        def sem(name):
            return ctx.enter_context(nc.semaphore(name))

        y = sb("y", [P, 2 * HEADS, SEQ])
        y_flat = y[:, :, :].rearrange("p a b -> p (a b)")
        raw = sb("raw", [P, 2, HALF * P])
        wh = sb("wh", [P, SLOTS, HALF * P], F32R)
        wl = sb("wl", [P, SLOTS, HALF * P], F32R)
        u = sb("u", [P, PAD + SEQ])
        tmp = sb("tmp", [P, SEQ])
        odd = sb("odd", [P, SEQ])
        csum = sb("csum", [P, SEQ])
        ident = sb("ident", [P, P])
        ident16 = sb("ident16", [P, P], BF16)
        mask16 = sb("mask16", [P, P], BF16)
        mean_w = sb("mean_w", [P, P])
        cols = sb("cols", [P, 7 * HEADS])
        hcols = sb("hcols", [P, 7 * HEADS])
        cn = sb("cn", [P, 3 * HEADS])
        hcn = sb("hcn", [P, 3 * HEADS])
        taps = sb("taps", [P, HEADS, TAPS])
        now = sb("now", [P, 6])
        now_z = sb("now_z", [P, 2])
        now_n = sb("now_n", [P, 2])
        fbias = sb("fbias", [HEADS, 1])
        one = sb("one", [P, 1])
        eps = sb("eps", [P, 1])
        row_max = sb("row_max", [P, NT])
        neg_max = sb("neg_max", [P, NT])
        row_sum = sb("row_sum", [P, NT])
        row_inv = sb("row_inv", [P, NT])
        stats = sb("stats", [P, 4, 6])
        mv = sb("mv", [P, 2])
        lnv = sb("lnv", [P, 1])
        rs = sb("rs", [P, 1])
        nt1 = sb("nt1", [P, 1])
        nt2 = sb("nt2", [P, 1])
        shift = sb("shift", [P, 1])

        first = ExitStack()
        parts = sb("parts", [P, 2 * PT_AT[NT]], F32R, first)
        v_t = sb("v_t", [P, SEQ], F32, first)
        vh = sb("vh", [P, NT * P], F32R, first)
        vl = sb("vl", [P, NT * P], F32R, first)
        probs = sb("probs", [P, PR_AT[NT]], F32, first)
        cum_q = sb("cum_q", [P, SEQ], F32R, first)
        cum_k = sb("cum_k", [P, SEQ], F32R, first)
        first.close()
        zbuf = sb("zbuf", [P, 4, SEQ])
        yh = sb("yh", [P, 2, SEQ], F32R)
        yl = sb("yl", [P, 2, SEQ], F32R)
        sq = sb("sq", [P, 3, SEQ])
        sq_odd = sb("sq_odd", [P, SEQ])
        rstd = sb("rstd", [P, SEQ])
        second = ExitStack()
        xh = sb("xh", [P, KT, SEQ], F32R, second)
        xl = sb("xl", [P, KT, SEQ], F32R, second)
        second.close()
        res = sb("res", [P, NT, D])
        bout_b = sb("bout_b", [P, D])
        gpost_b = sb("gpost_b", [P, D])
        bpost_b = sb("bpost_b", [P, D])

        ps = ctx.enter_context(nc.psum_tensor("ps", [P, 8, SEQ], F32))
        S0, V_BANK, O_BANK = 2, 6, 7
        qh, ql, kh, kl = (parts[:, SEQ * n:SEQ * (n + 1)] for n in range(4))
        pth, ptl = parts[:, 0:PT_AT[NT]], parts[:, PT_AT[NT]:]
        x_rows = y_flat[:, 0:NT * D].rearrange("p (t d) -> p t d", t=NT)
        rows = y_flat[:, NT * D:]
        cum4 = y_flat[0:HEADS, 12 * SEQ:16 * SEQ]
        fz, fa = probs[0:HEADS, 0:SEQ], probs[0:HEADS, SEQ:2 * SEQ]
        fm, fcum = v_t[0:HEADS, :], tmp[0:HEADS, :]

        x_loaded = [sem(f"x_loaded{c}") for c in range(4)]
        rows_loaded, bcast_loaded, stored = sem("rows_loaded"), sem("bcast_loaded"), sem("stored")
        raw_full = [sem("raw_full0"), sem("raw_full1")]
        cum_stored, cum_loaded = sem("cum_stored"), sem("cum_loaded")
        res_loaded = sem("res_loaded")
        const_done, vec_const = sem("const_done"), sem("vec_const")
        xt_turned, xh_done, xl_done = sem("xt_turned"), sem("xh_done"), sem("xl_done")
        cols_turned, cols_done = sem("cols_turned"), sem("cols_done")
        high_done, low_done, half_done = sem("high_done"), sem("low_done"), sem("half_done")
        f_act, f_vec = sem("f_act"), sem("f_vec")
        qk_high, qk_low = sem("qk_high"), sem("qk_low")
        vt_done, v_turned, vh_done, vl_done = sem("vt_done"), sem("v_turned"), sem("vh_done"), sem("vl_done")
        scores_done, max_done, negmax_done = sem("scores_done"), sem("max_done"), sem("negmax_done")
        exp_done, inv_done, probs_done = sem("exp_done"), sem("inv_done"), sem("probs_done")
        p_turned, pth_done, ptl_done, pv_done = sem("p_turned"), sem("pth_done"), sem("ptl_done"), sem("pv_done")
        now_done, nowz_done, nown_done = sem("now_done"), sem("nowz_done"), sem("nown_done")
        gate_read, gate_done, attn_done = sem("gate_read"), sem("gate_done"), sem("attn_done")
        val_read, glu_tanh, u_done, tap_done = sem("val_read"), sem("glu_tanh"), sem("u_done"), sem("tap_done")
        conv_done, csum_done, mean_done = sem("conv_done"), sem("csum_done"), sem("mean_done")
        cent_done, sq_done, sqe_done, sqo_done = sem("cent_done"), sem("sq_done"), sem("sqe_done"), sem("sqo_done")
        var_done, rstd_act, rstd_vec = sem("var_done"), sem("rstd_act"), sem("rstd_vec")
        z_read, z_done = sem("z_read"), sem("z_done")
        norm_done, aff_done, act_done, yc_done = sem("norm_done"), sem("aff_done"), sem("act_done"), sem("yc_done")
        yh_done, yl_done = sem("yh_done"), sem("yl_done")
        res_scaled, res_ready, evac_done = sem("res_scaled"), sem("res_ready"), sem("evac_done")
        fin_vec, fin_act, row_done = sem("fin_vec"), sem("fin_act"), sem("row_done")
        fin_pool = sem("fin_pool")

        block = ctx.enter_context(nc.Block())

        def ds(i, n):
            return bass.ds(i, n)

        @block.sync
        def _(sp):
            def load_in(t, col, second_first=False):
                for h in (1, 0) if second_first else (0, 1):
                    if not (isinstance(t, int) and t == 0) and not (second_first and h == 0):
                        sp.wait_ge(low_done, 2 * t + h - 1)
                    src = w_in[D // 2 * h:D // 2 * (h + 1), ds(col, P)]
                    sp.dma_start(raw[:, h, :].rearrange("p (k c) -> p k c", k=HALF),
                                 src.rearrange("(k p) c -> p k c", p=P)).then_inc(raw_full[h], 16)

            def load_out(t, row, half_cols):
                for h in range(2):
                    sp.wait_ge(low_done, 2 * t + h - 1)
                    sp.dma_start(raw[:, h, :], w_out[ds(row + P * h, P), half_cols * 1024:half_cols * 1024 + 1024]) \
                      .then_inc(raw_full[h], 16)

            def load_cum(h):
                sp.dma_start(cum_q[0:2, :].bitcast(F32),
                             scratch[ds(h, 1), 0:2 * SEQ].rearrange("a (r n) -> (a r) n", r=2)).then_inc(cum_loaded, 16)
                sp.dma_start(cum_k[2:4, :].bitcast(F32),
                             scratch[ds(h, 1), 2 * SEQ:4 * SEQ].rearrange("a (r n) -> (a r) n", r=2)).then_inc(cum_loaded, 16)

            x_v = x.rearrange("a (t p) d -> p (a t) d", p=P)
            for c in range(4):
                sp.dma_start(x_rows[:, :, SEQ * c:SEQ * (c + 1)], x_v[:, :, SEQ * c:SEQ * (c + 1)]) \
                  .then_inc(x_loaded[c], 16)
                if c == 0:
                    load_in(0, F_COL)
            sp.dma_start(rows[0:TAPS, 0:D], w_dw).then_inc(rows_loaded, 16)
            sp.dma_start(rows[0:6 * HEADS, D:D + P], b_in[0:6 * D].rearrange("(j p) -> j p", p=P)).then_inc(rows_loaded, 16)
            sp.dma_start(rows[6 * HEADS:7 * HEADS, D:D + P],
                         b_in[F_COL + HEADS:F_COL + HEADS + D].rearrange("(j p) -> j p", p=P)).then_inc(rows_loaded, 16)
            for n, vec in enumerate((b_dw, g_cn, b_cn)):
                sp.dma_start(rows[n * HEADS:(n + 1) * HEADS, D + P:D + 2 * P],
                             vec.rearrange("(j p) -> j p", p=P)).then_inc(rows_loaded, 16)
            sp.dma_start(fbias[:, :], b_in[F_COL:F_COL + HEADS].rearrange("(j p) -> j p", p=1)).then_inc(rows_loaded, 16)
            load_in(1, col_of(Q, 0))

            def body(i):
                for s, kind in enumerate(BODY_KINDS):
                    t = i * PER_HEAD + (T_BODY + s)
                    if s + 1 < PER_HEAD:
                        load_in(t + 1, col_of(BODY_KINDS[s + 1], 0) + i * P, BODY_KINDS[s + 1] == VAL)
                    if s == 1 and isinstance(i, int):
                        sp.wait_ge(f_vec, 7)
                        sp.dma_start(scratch, cum4).then_inc(cum_stored, 16)
                        sp.wait_ge(cum_stored, 16)
                        sp.wait_ge(const_done, 8)
                        load_cum(0)

            def next_cum(i):
                sp.wait_ge(scores_done, i * NT + NT)
                load_cum(i + 1)

            body(0)
            next_cum(0)
            load_in(T_BODY + PER_HEAD, col_of(Q, 1))
            with nc.sync.Fori(1, HEADS - 1) as i:
                body(i)
                next_cum(i)
                load_in(i * PER_HEAD + (T_BODY + PER_HEAD), col_of(Q, 1) + i * P)
            i = HEADS - 1
            for s in range(1, PER_HEAD):
                load_in(T_BODY + i * PER_HEAD + s, col_of(BODY_KINDS[s], i))
            with nc.sync.Fori(0, HEADS) as j:
                load_in(j + T_GATE, col_of(GATE_C, 0) + j * P)
            for p in range(2):
                t = T_OUT + p * OUT_PAIRS
                with nc.sync.Fori(0, OUT_PAIRS // 2) as m:
                    load_out(m + t, D + m * (2 * P), p)
                with nc.sync.Fori(0, OUT_PAIRS // 2) as m:
                    load_out(m + (t + OUT_PAIRS // 2), m * (2 * P), p)
            for t in range(NT):
                sp.wait_ge(row_done, 2 * (t + 1))
                sp.dma_start(out[0, P * t:P * (t + 1), :], res[:, t, :]).then_inc(stored, 16)
            sp.wait_ge(stored, 16 * NT)

        @block.gpsimd
        def _(pool):
            nc.gpsimd.memset(ident[:, :], 0.0).then_inc(const_done, 1)
            nc.gpsimd.memset(ident16[:, :], 0.0).then_inc(const_done, 1)
            nc.gpsimd.memset(mask16[:, :], 0.0).then_inc(const_done, 1)
            pool.wait_ge(const_done, 3)
            nc.gpsimd.affine_select(out=ident[:, :], in_=ident[:, :], compare_op=ALU.not_equal, fill=1.0,
                                    base=0, pattern=[[-1, P]], channel_multiplier=1).then_inc(const_done, 1)
            nc.gpsimd.affine_select(out=ident16[:, :], in_=ident16[:, :], compare_op=ALU.not_equal, fill=1.0,
                                    base=0, pattern=[[-1, P]], channel_multiplier=1).then_inc(const_done, 1)
            nc.gpsimd.affine_select(out=mask16[:, :], in_=mask16[:, :], compare_op=ALU.is_ge, fill=MASKED,
                                    base=0, pattern=[[-1, P]], channel_multiplier=1).then_inc(const_done, 1)
            pool.wait_ge(vec_const, 4)
            nc.gpsimd.memset(cum_q[0:4, :].bitcast(F32), 1.0).then_inc(const_done, 1)
            nc.gpsimd.memset(cum_k[0:4, :].bitcast(F32), 1.0).then_inc(const_done, 1)

            pool.wait_ge(vec_const, 6)

            pool.wait_ge(conv_done, 1)
            nc.gpsimd.tensor_tensor(csum[:, :], csum[:, :], y[:, HEADS, :], ALU.add).then_inc(csum_done, 1)
            with nc.gpsimd.Fori(1, HEADS) as i:
                pool.wait_ge(conv_done, i + 1)
                pool.wait_ge(csum_done, i)
                nc.gpsimd.tensor_tensor(csum[:, :], csum[:, :], y[:, ds(HEADS + i, 1), :].rearrange("p a b -> p (a b)"),
                                        ALU.add).then_inc(csum_done, 1)
            pool.wait_ge(mean_done, 1)
            nc.gpsimd.memset(csum[:, :], 0.0).then_inc(sqe_done, 1)
            for j in range(0, HEADS, 2):
                pool.wait_ge(sq_done, j + 1)
                pool.wait_ge(sqe_done, j // 2 + 1)
                nc.gpsimd.tensor_tensor(csum[:, :], csum[:, :], sq[:, j % 3, :], ALU.add).then_inc(sqe_done, 1)

            pool.wait_ge(half_done, 2 * T_OUT)
            with nc.allow_non_contiguous_dma(reason="rows repeated over the partitions"):
                for dst, src in ((bout_b, b_out), (gpost_b, g_post), (bpost_b, b_post)):
                    nc.gpsimd.dma_start(dst[:, :], src.partition_broadcast(P)).then_inc(bcast_loaded, 16)
            for t in range(NT):
                nc.gpsimd.dma_start(res[:, t, :], x[0, P * t:P * (t + 1), :]).then_inc(res_loaded, 16)
            pool.wait_ge(res_loaded, 16 * NT)
            pool.wait_ge(bcast_loaded, 48)
            for t in range(NT):
                nc.gpsimd.tensor_scalar(res[:, t, :], res[:, t, :], ALPHA, None, ALU.mult).then_inc(res_scaled, 1)
                pool.wait_ge(res_scaled, t + 1)
                nc.gpsimd.tensor_tensor(res[:, t, :], res[:, t, :], bout_b[:, :], ALU.add).then_inc(res_ready, 1)

        @block.scalar
        def _(act):
            def high(t, par, h, lag=4):
                act.wait_ge(raw_full[h], 16 * (t + 1))
                if not isinstance(t, int) or t >= 2:
                    act.wait_ge(half_done, 2 * t + (h + 1 - lag))
                nc.scalar.activation(wh[:, 2 * par + h, :], raw[:, h, :], ACT.Copy).then_inc(high_done, 1)

            def bank_of(par):
                return ps[:, par, :]

            def bias_of(kind):
                return now[:, NOW[kind][0]:NOW[kind][0] + 1]

            def tile_done(t):
                act.wait_ge(half_done, 2 * t + 2)

            def x_high(kt):
                act.wait_ge(xt_turned, kt + 1)
                nc.scalar.activation(xh[:, kt, :], ps[:, S0 + kt % 4, :], ACT.Copy).then_inc(xh_done, 1)

            for kt in range(HALF):
                x_high(kt)
            high(0, 0, 0)
            high(0, 0, 1)
            for kt in range(HALF, KT):
                x_high(kt)
            high(1, 1, 0)
            high(1, 1, 1)
            act.wait_ge(cols_turned, 1)
            nc.scalar.activation(cols[:, :], ps[:, V_BANK, 0:7 * HEADS], ACT.Copy).then_inc(cols_done, 1)
            nc.scalar.activation(hcols[:, :], ps[:, V_BANK, 0:7 * HEADS], ACT.Copy, scale=0.5).then_inc(cols_done, 1)
            nc.scalar.activation(cn[:, :], ps[:, V_BANK, 128:128 + 3 * HEADS], ACT.Copy).then_inc(cols_done, 1)
            nc.scalar.activation(hcn[:, :], ps[:, V_BANK, 128:128 + 3 * HEADS], ACT.Copy, scale=0.5).then_inc(cols_done, 1)
            act.wait_ge(cols_turned, 2)
            nc.scalar.activation(taps[:, :, :].rearrange("p a b -> p (a b)"), ps[:, O_BANK, 0:HEADS * TAPS],
                                 ACT.Copy).then_inc(cols_done, 1)
            act.wait_ge(cols_done, 5)

            tile_done(0)
            act.wait_ge(rows_loaded, 16 * 7)
            act.wait_ge(vec_const, 6)
            nc.scalar.activation(fz, ps[0:HEADS, 0, :], ACT.Identity, bias=fbias[:, :]).then_inc(f_act, 1)
            nc.scalar.activation(fa, ps[0:HEADS, 0, :], ACT.Abs, bias=fbias[:, :]).then_inc(f_act, 1)
            act.wait_ge(f_act, 2)
            nc.scalar.activation(fa, fa, ACT.Exp, scale=-1.0).then_inc(f_act, 1)
            act.wait_ge(f_act, 3)
            nc.scalar.activation(fa, fa, ACT.Ln, bias=one[0:HEADS, :]).then_inc(f_act, 1)
            act.wait_ge(f_vec, 3)
            nc.scalar.activation(cum4[:, 0:SEQ].bitcast(F32R), fcum, ACT.Copy).then_inc(f_act, 1)

            def glu_gate(t, i):
                tile_done(t)
                act.wait_ge(gate_done, i + 1)
                nc.scalar.activation(tmp[:, :], bank_of(0), ACT.Tanh, bias=bias_of(GLU), scale=0.5) \
                  .then_inc(glu_tanh, 1)

            def body(i, i0):
                t = i * PER_HEAD + T_BODY
                if not i0:
                    glu_gate(t - 1, i - 1)
                high(t + 1, 0, 0)
                high(t + 1, 0, 1)
                tile_done(t)
                if not i0:
                    act.wait_ge(pv_done, i)
                act.wait_ge(now_done, i + 1)
                nc.scalar.activation(qh, bank_of(1), ACT.Identity, bias=bias_of(Q)).then_inc(qk_high, 1)
                high(t + 2, 1, 0)
                high(t + 2, 1, 1)
                tile_done(t + 1)
                nc.scalar.activation(kh, bank_of(0), ACT.Identity, bias=bias_of(K)).then_inc(qk_high, 1)
                high(t + 3, 0, 0)
                high(t + 3, 0, 1)
                act.wait_ge(negmax_done, i + 1)
                for b in range(NT):
                    nc.scalar.activation(probs[:, PR_AT[b]:PR_AT[b + 1]], ps[:, S0 + b, 0:P * (b + 1)], ACT.Exp,
                                         bias=neg_max[:, b:b + 1], scale=SCALE,
                                         accum_out=row_sum[:, b:b + 1]).then_inc(exp_done, 1)
                tile_done(t + 2)
                nc.scalar.activation(v_t[:, :], bank_of(1), ACT.Identity, bias=bias_of(V)).then_inc(vt_done, 1)
                high(t + 4, 1, 0)
                high(t + 4, 1, 1)
                act.wait_ge(v_turned, i + 1)
                nc.scalar.activation(vh[:, :], ps[:, V_BANK, :], ACT.Copy).then_inc(vh_done, 1)
                tile_done(t + 3)
                nc.scalar.activation(v_t[:, :], bank_of(0), ACT.Identity,
                                     bias=bias_of(GATE_A), scale=0.5).then_inc(gate_read, 1)
                if not i0:
                    act.wait_ge(u_done, i)
                nc.scalar.activation(tmp[:, :], bank_of(0), ACT.Tanh, bias=bias_of(GATE_A), scale=0.5) \
                  .then_inc(gate_read, 1)
                high(t + 5, 0, 0)
                high(t + 5, 0, 1)
                for j in range(NT):
                    act.wait_ge(p_turned, i * NT + (j + 1))
                    nc.scalar.activation(pth[:, PT_AT[j]:PT_AT[j + 1]], ps[:, S0 + j, 0:PT_N[j]], ACT.Copy) \
                      .then_inc(pth_done, 1)
                tile_done(t + 4)
                if not i0:
                    act.wait_ge(conv_done, i)
                act.wait_ge(vec_const, 6)
                nc.scalar.activation(u[:, PAD:], bank_of(1), ACT.Identity, bias=bias_of(VAL), scale=0.5) \
                  .then_inc(val_read, 1)
                high(t + 6, 1, 0)
                high(t + 6, 1, 1)

            body(0, True)
            with nc.scalar.Fori(1, HEADS) as i:
                body(i, False)

            def gate_c(t, j, slot, par):
                tile_done(t)
                act.wait_ge(attn_done, HEADS)
                act.wait_ge(nowz_done, j + 1)
                if not isinstance(j, int) or j >= 4:
                    act.wait_ge(yc_done, j - 3)
                nc.scalar.activation(zbuf[:, slot, :], bank_of(par), ACT.Identity,
                                     bias=now_z[:, par:par + 1], scale=0.5).then_inc(z_read, 1)
                if isinstance(j, int) and j == 0:
                    act.wait_ge(u_done, HEADS)
                else:
                    act.wait_ge(z_done, j)
                nc.scalar.activation(tmp[:, :], bank_of(par), ACT.Tanh,
                                     bias=now_z[:, par:par + 1], scale=0.5).then_inc(z_read, 1)

            def finish_conv(j, slot):
                act.wait_ge(norm_done, j + 1)
                if not isinstance(j, int) or j:
                    act.wait_ge(act_done, j)
                nc.scalar.activation(odd[:, :], sq[:, 0, :], ACT.Tanh, bias=now_n[:, 1:2], scale=now_n[:, 0:1]) \
                  .then_inc(aff_done, 1)
                nc.scalar.activation(sq[:, 1, :], sq[:, 0, :], ACT.Identity, bias=now_n[:, 1:2],
                                     scale=now_n[:, 0:1]).then_inc(aff_done, 1)

            t = T_GATE
            glu_gate(t - 1, HEADS - 1)
            high(t + 1, 0, 0)
            high(t + 1, 0, 1)
            gate_c(t, 0, 0, 1)
            high(t + 2, 1, 0)
            high(t + 2, 1, 1)
            gate_c(t + 1, 1, 1, 0)
            high(t + 3, 0, 0)
            high(t + 3, 0, 1)
            for j in range(HEADS):
                act.wait_ge(cent_done, j + 1)
                if j >= 3:
                    act.wait_ge(sqo_done if j % 2 == 0 else sqe_done, (j - 3) // 2 + 2)
                nc.scalar.activation(sq[:, j % 3, :], y[:, HEADS + j, :], ACT.Square).then_inc(sq_done, 1)
                if j == 7:
                    gate_c(t + 2, 2, 2, 1)
                    high(t + 4, 1, 0)
                    high(t + 4, 1, 1)
            act.wait_ge(rstd_vec, 1)
            nc.scalar.activation(odd[:, :], sq_odd[:, :], ACT.Ln).then_inc(rstd_act, 1)
            act.wait_ge(rstd_act, 1)
            nc.scalar.activation(rstd[:, :], odd[:, :], ACT.Exp, scale=-0.5).then_inc(rstd_act, 1)

            def gate_step(j, s):
                gate_c(j + (T_GATE - 1), j - 1, (s - 1) % 4, s % 2)
                high(j + (T_GATE + 1), s % 2, 0)
                finish_conv(j - 4, s)
                high(j + (T_GATE + 1), s % 2, 1)

            with nc.scalar.Fori(1, HEADS // 4) as b:
                for s in range(4):
                    gate_step(b * 4 + s, s)

            def y_tile(k):
                return y[:, ds(k, 1), :].rearrange("p a b -> p (a b)")

            def split_y(slot, src):
                nc.scalar.activation(yh[:, slot, :], src, ACT.Copy).then_inc(yh_done, 1)

            def out_pair(pair, m, s, nxt):
                t = pair + T_OUT
                high(t + 1, s, 0, lag=3)
                split_y(1, y_tile(m * 2 + 1))
                high(t + 1, s, 1, lag=3)
                split_y(0, y_tile(nxt))

            act.wait_ge(attn_done, HEADS)
            split_y(0, y_tile(0))
            gate_c(T_OUT - 1, HEADS - 1, 3, 0)
            out_pair(0, 0, 0, 2)
            finish_conv(HEADS - 4, 0)
            finish_conv(HEADS - 3, 1)
            out_pair(1, 1, 1, 4)
            finish_conv(HEADS - 2, 2)
            finish_conv(HEADS - 1, 3)
            with nc.scalar.Fori(1, OUT_PAIRS // 4) as b:
                for s in range(2):
                    out_pair(b * 2 + s, b * 2 + s, s, b * 4 + (2 * s + 2))
            act.wait_ge(yc_done, HEADS)
            with nc.scalar.Fori(OUT_PAIRS // 4, OUT_PAIRS // 2 - 1) as b:
                for s in range(2):
                    out_pair(b * 2 + s, b * 2 + s, s, b * 4 + (2 * s + 2))
            out_pair(OUT_PAIRS - 2, OUT_PAIRS - 2, 0, 2 * OUT_PAIRS - 2)
            out_pair(OUT_PAIRS - 1, OUT_PAIRS - 1, 1, 0)
            with nc.scalar.Fori(0, OUT_PAIRS // 2 - 1) as b:
                for s in range(2):
                    out_pair(b * 2 + (OUT_PAIRS + s), b * 2 + s, s, b * 4 + (2 * s + 2))
            out_pair(N_OUT - 2, OUT_PAIRS - 2, 0, 2 * OUT_PAIRS - 2)
            act.wait_ge(half_done, 2 * T_OUT + 2 * N_OUT - 2)
            split_y(1, y_tile(2 * OUT_PAIRS - 1))

            for t in range(NT):
                act.wait_ge(fin_vec, 12 * t + 4 + 3)
                nc.scalar.activation(lnv[:, :], mv[:, 1:2], ACT.Ln).then_inc(fin_act, 1)
                act.wait_ge(fin_act, 4 * t + 1)
                nc.scalar.activation(rs[:, :], lnv[:, :], ACT.Exp, scale=-0.5).then_inc(fin_act, 1)
                act.wait_ge(fin_vec, 12 * t + 12)
                for h in range(2):
                    nc.scalar.activation(res[:, t, h * 1024:(h + 1) * 1024], res[:, t, h * 1024:(h + 1) * 1024],
                                         ACT.Identity, bias=shift[:, :], scale=rs[:, :]).then_inc(fin_act, 1)

        @block.tensor
        def _(pe):
            def mm3(o, ah, al, bh, bl, start):
                nc.tensor.matmul(o, ah, bh, start=start, stop=False, skip_group_check=True)
                nc.tensor.matmul(o, ah, bl, start=False, stop=False, skip_group_check=True)
                return nc.tensor.matmul(o, al, bh, start=False, stop=True, skip_group_check=True)

            def half(t, par, h):
                pe.wait_ge(low_done, 2 * t + (h + 1))
                for k in range(HALF):
                    a = slice(P * k, P * (k + 1))
                    last = mm3(ps[:, par, :], wh[:, 2 * par + h, a], wl[:, 2 * par + h, a],
                               xh[:, HALF * h + k, :], xl[:, HALF * h + k, :], h == 0 and k == 0)
                last.then_inc(half_done, 1)

            pe.wait_ge(const_done, 6)
            for kt in range(KT):
                if kt % 4 == 0:
                    pe.wait_ge(x_loaded[kt // 4], 16)
                if kt >= 4:
                    pe.wait_ge(xl_done, kt - 3)
                for n in range(NT):
                    last = nc.tensor.transpose(ps[:, S0 + kt % 4, P * n:P * (n + 1)],
                                               x_rows[:, n, P * kt:P * (kt + 1)], ident[:, :])
                last.then_inc(xt_turned, 1)
            pe.wait_ge(rows_loaded, 16 * 7)
            nc.tensor.transpose(ps[:, V_BANK, 0:7 * HEADS], rows[0:7 * HEADS, D:D + P], ident[0:7 * HEADS, 0:7 * HEADS])
            nc.tensor.transpose(ps[:, V_BANK, 128:128 + 3 * HEADS], rows[0:3 * HEADS, D + P:D + 2 * P],
                                ident[0:3 * HEADS, 0:3 * HEADS]).then_inc(cols_turned, 1)
            for c in range(HEADS):
                last = nc.tensor.transpose(ps[:, O_BANK, TAPS * c:TAPS * (c + 1)], rows[0:TAPS, P * c:P * (c + 1)],
                                           ident[0:TAPS, 0:TAPS])
            last.then_inc(cols_turned, 1)
            pe.wait_ge(xl_done, HALF)
            half(0, 0, 0)
            pe.wait_ge(xl_done, KT)
            half(0, 0, 1)

            def body(i, i0):
                t = i * PER_HEAD + T_BODY
                if not i0:
                    pe.wait_ge(val_read, i)
                half(t, 1, 0)
                half(t, 1, 1)
                if i0:
                    pe.wait_ge(f_act, 2)
                else:
                    pe.wait_ge(glu_tanh, i)
                half(t + 1, 0, 0)
                half(t + 1, 0, 1)
                pe.wait_ge(qk_low, i * 2 + 1)
                half(t + 2, 1, 0)
                pe.wait_ge(qk_low, i * 2 + 2)
                pe.wait_ge(cum_loaded, i * 32 + 32)
                if not i0:
                    pe.wait_ge(ptl_done, i * NT)
                for b in range(NT):
                    o, m, c = ps[:, S0 + b, 0:P * (b + 1)], slice(P * b, P * (b + 1)), slice(0, P * (b + 1))
                    nc.tensor.matmul(o, cum_q[:, m], cum_k[:, c], start=True, stop=False, skip_group_check=True)
                    nc.tensor.matmul(ps[:, S0 + b, m], ident16[:, :], mask16[:, :], start=False, stop=False,
                                     skip_group_check=True)
                    mm3(o, qh[:, m], ql[:, m], kh[:, c], kl[:, c], False).then_inc(scores_done, 1)
                half(t + 2, 1, 1)
                half(t + 3, 0, 0)
                pe.wait_ge(vt_done, i + 1)
                if not i0:
                    pe.wait_ge(vl_done, i)
                for b in range(NT):
                    last = nc.tensor.transpose(ps[:, V_BANK, P * b:P * (b + 1)], v_t[:, P * b:P * (b + 1)], ident[:, :])
                last.then_inc(v_turned, 1)
                half(t + 3, 0, 1)
                half(t + 4, 1, 0)
                pe.wait_ge(probs_done, i * NT + NT)
                for j in range(NT):
                    for b in range(j, NT):
                        last = nc.tensor.transpose(ps[:, S0 + j, P * (b - j):P * (b - j + 1)],
                                                   probs[:, PR_AT[b] + P * j:PR_AT[b] + P * (j + 1)], ident[:, :])
                    last.then_inc(p_turned, 1)
                half(t + 4, 1, 1)
                pe.wait_ge(gate_read, i * 2 + 2)
                half(t + 5, 0, 0)
                pe.wait_ge(ptl_done, i * NT + NT)
                pe.wait_ge(vl_done, i + 1)
                if not i0:
                    pe.wait_ge(attn_done, i)
                for j in range(NT):
                    a, c = slice(P * j, P * (j + 1)), slice(PT_AT[j], PT_AT[j + 1])
                    last = mm3(ps[:, O_BANK, P * j:SEQ], vh[:, a], vl[:, a], pth[:, c], ptl[:, c], j == 0)
                last.then_inc(pv_done, 1)
                half(t + 5, 0, 1)

            body(0, True)
            with nc.tensor.Fori(1, HEADS) as i:
                body(i, False)

            for j in range(4):
                if j == 0:
                    pe.wait_ge(val_read, HEADS)
                elif j == 1:
                    pe.wait_ge(glu_tanh, HEADS)
                else:
                    pe.wait_ge(z_read, 2 * j - 2)
                half(T_GATE + j, (j + 1) % 2, 0)
                if j == 2:
                    pe.wait_ge(csum_done, HEADS)
                    pe.wait_ge(vl_done, HEADS)
                    nc.tensor.matmul(ps[:, V_BANK, :], mean_w[:, :], csum[:, :], start=True, stop=True) \
                      .then_inc(mean_done, 1)
                half(T_GATE + j, (j + 1) % 2, 1)
            pe.wait_ge(sqe_done, HEADS // 2 + 1)
            pe.wait_ge(sqo_done, HEADS // 2 + 1)
            pe.wait_ge(attn_done, HEADS)
            nc.tensor.matmul(ps[:, O_BANK, :], mean_w[:, :], csum[:, :], start=True, stop=False)
            nc.tensor.matmul(ps[:, O_BANK, :], mean_w[:, :], sq_odd[:, :], start=False, stop=True).then_inc(var_done, 1)
            with nc.tensor.Fori(1, HEADS // 4) as b:
                for s in range(4):
                    pe.wait_ge(z_read, b * 8 + (2 * s - 2))
                    half(b * 4 + (T_GATE + s), (s + 1) % 2, 0)
                    half(b * 4 + (T_GATE + s), (s + 1) % 2, 1)

            def bank(n, g):
                return (2 * n + g + 2) % 8

            def ready(step):
                pe.wait_ge(low_done, step + (2 * T_OUT + 1))
                pe.wait_ge(yl_done, step + 1)

            def slot_of(q):
                return (2 * T_OUT + q) % SLOTS

            Y_SLOT = [0, 1, 0, 1]

            def step_mm(step, q, tokens=range(NT), begin=False):
                for n in tokens:
                    for g in range(2):
                        a, c = slice(P * n, P * (n + 1)), slice(SEQ * g, SEQ * (g + 1))
                        last = mm3(ps[:, bank(n, g), :], yh[:, Y_SLOT[q], a], yl[:, Y_SLOT[q], a],
                                   wh[:, slot_of(q), c], wl[:, slot_of(q), c], begin)
                return last

            per_pass = 2 * OUT_PAIRS
            for p in range(2):
                at = p * per_pass
                ready(at)
                if p == 0:
                    pe.wait_ge(rstd_vec, 2)
                    pe.wait_ge(cent_done, HEADS)
                    pe.wait_ge(ptl_done, HEADS * NT)
                for n in range(NT):
                    for g in range(2):
                        if p == 0 and bank(n, g) < 2:
                            pe.wait_ge(z_read, 2 * HEADS)
                        if p == 1:
                            pe.wait_ge(evac_done, 2 * n + g + 1)
                        a, c = slice(P * n, P * (n + 1)), slice(SEQ * g, SEQ * (g + 1))
                        last = mm3(ps[:, bank(n, g), :], yh[:, 0, a], yl[:, 0, a],
                                   wh[:, slot_of(0), c], wl[:, slot_of(0), c], True)
                last.then_inc(half_done, 1)
                for q in range(1, 4):
                    ready(at + q)
                    step_mm(at + q, q).then_inc(half_done, 1)
                end = OUT_PAIRS // 2 - (1 if p == 1 else 0)
                with nc.tensor.Fori(1, end) as b:
                    for q in range(4):
                        ready(b * 4 + (at + q))
                        step_mm(b * 4 + (at + q), q).then_inc(half_done, 1)
            for q in range(2):
                ready(2 * per_pass - 4 + q)
                step_mm(2 * per_pass - 4 + q, q).then_inc(half_done, 1)
            ready(2 * per_pass - 2)
            ready(2 * per_pass - 1)
            for n in range(NT):
                step_mm(2 * per_pass - 2, 2, [n])
                step_mm(2 * per_pass - 1, 3, [n]).then_inc(half_done, 1)

        @block.vector
        def _(dve):
            vec = nc.vector

            def low(t, par, h):
                dve.wait_ge(high_done, 2 * t + (h + 1))
                vec.tensor_tensor(wl[:, 2 * par + h, :], raw[:, h, :], wh[:, 2 * par + h, :], ALU.subtract) \
                   .then_inc(low_done, 1)

            def col(table, kind, i):
                return table[:, ds(kind * HEADS + i, 1)]

            def y_tile(k):
                return y[:, ds(k, 1), :].rearrange("p a b -> p (a b)")

            vec.memset(mean_w[:, :], 1.0 / D).then_inc(vec_const, 1)
            vec.memset(one[:, :], 1.0).then_inc(vec_const, 1)
            vec.memset(cum_q[:, :].bitcast(F32), 0.0).then_inc(vec_const, 1)
            vec.memset(cum_k[:, :].bitcast(F32), 0.0).then_inc(vec_const, 1)
            vec.memset(u[:, 0:PAD], 0.0).then_inc(vec_const, 1)
            vec.memset(csum[:, :], 0.0).then_inc(vec_const, 1)

            def x_low(kt):
                dve.wait_ge(xh_done, kt + 1)
                vec.tensor_tensor(xl[:, kt, :], ps[:, S0 + kt % 4, :], xh[:, kt, :], ALU.subtract).then_inc(xl_done, 1)

            for kt in range(HALF):
                x_low(kt)
            low(0, 0, 0)
            low(0, 0, 1)
            for kt in range(HALF, KT):
                x_low(kt)
            low(1, 1, 0)
            low(1, 1, 1)
            dve.wait_ge(cols_done, 5)

            def conv(i, n0, n1):
                for w in range(n0, n1):
                    o = odd[:, :] if w % 2 else y_tile(HEADS + i)
                    if w > 1:
                        dve.wait_ge(tap_done, i * TAPS + (w - 1))
                    tap = taps[:, ds(i, 1), w]
                    if w == 0:
                        ins = vec.tensor_scalar(o, u[:, 0:SEQ], tap, col(cn, B_DW, i), ALU.mult, ALU.add)
                    elif w == 1:
                        if not isinstance(i, int) or i:
                            dve.wait_ge(conv_done, i)
                        ins = vec.tensor_scalar(o, u[:, w:w + SEQ], tap, None, ALU.mult)
                    else:
                        ins = vec.scalar_tensor_tensor(out=o, in0=u[:, w:w + SEQ], scalar=tap, in1=o,
                                                       op0=ALU.mult, op1=ALU.add)
                    ins.then_inc(tap_done, 1)

            def conv_end(i):
                dve.wait_ge(tap_done, i * TAPS + TAPS)
                vec.tensor_tensor(y_tile(HEADS + i), y_tile(HEADS + i), odd[:, :], ALU.add).then_inc(conv_done, 1)

            def glu(i):
                dve.wait_ge(val_read, i + 1)
                dve.wait_ge(glu_tanh, i + 1)
                vec.scalar_tensor_tensor(out=u[:, PAD:], in0=tmp[:, :], scalar=1.0, in1=u[:, PAD:],
                                         op0=ALU.add, op1=ALU.mult).then_inc(u_done, 1)
                dve.wait_ge(u_done, i + 1)

            def body(i, i0):
                t = i * PER_HEAD + T_BODY
                at = [sum(BODY_TAPS[:s]) for s in range(PER_HEAD + 1)]

                def taps_of(s, part):
                    if i0:
                        return
                    mid = (at[s] + at[s + 1] + 1) // 2
                    lo, hi = (at[s], mid) if part == 0 else (mid, at[s + 1])
                    conv(i - 1, lo, min(hi, TAPS))
                    if lo < TAPS <= hi:
                        conv_end(i - 1)

                if i0:
                    forget()
                else:
                    glu(i - 1)
                for kind, (at_col, halved) in NOW.items():
                    ins = vec.tensor_copy(now[:, at_col:at_col + 1], col(hcols if halved else cols, kind, i))
                ins.then_inc(now_done, 1)
                low(t + 1, 0, 0)
                taps_of(0, 0)
                low(t + 1, 0, 1)
                taps_of(0, 1)
                dve.wait_ge(qk_high, i * 2 + 1)
                vec.scalar_tensor_tensor(out=ql, in0=ps[:, 1, :], scalar=col(cols, Q, i), in1=qh,
                                         op0=ALU.add, op1=ALU.subtract).then_inc(qk_low, 1)
                low(t + 2, 1, 0)
                taps_of(1, 0)
                low(t + 2, 1, 1)
                taps_of(1, 1)
                dve.wait_ge(qk_high, i * 2 + 2)
                vec.scalar_tensor_tensor(out=kl, in0=ps[:, 0, :], scalar=col(cols, K, i), in1=kh,
                                         op0=ALU.add, op1=ALU.subtract).then_inc(qk_low, 1)
                low(t + 3, 0, 0)
                taps_of(2, 0)
                low(t + 3, 0, 1)
                if not i0:
                    dve.wait_ge(negmax_done, i)
                for b in range(NT):
                    dve.wait_ge(scores_done, i * NT + (b + 1))
                    vec.reduce_max(row_max[:, b:b + 1], ps[:, S0 + b, 0:P * (b + 1)], AX.X).then_inc(max_done, 1)
                dve.wait_ge(max_done, i * NT + NT)
                vec.tensor_scalar(neg_max[:, :], row_max[:, :], -SCALE, None, ALU.mult).then_inc(negmax_done, 1)
                taps_of(2, 1)
                dve.wait_ge(exp_done, i * NT + NT)
                vec.reciprocal(row_inv[:, :], row_sum[:, :]).then_inc(inv_done, 1)
                dve.wait_ge(inv_done, i + 1)
                for b in range(NT):
                    pr = probs[:, PR_AT[b]:PR_AT[b + 1]]
                    vec.tensor_scalar(pr, pr, row_inv[:, b:b + 1], None, ALU.mult).then_inc(probs_done, 1)
                low(t + 4, 1, 0)
                taps_of(3, 0)
                low(t + 4, 1, 1)
                dve.wait_ge(vh_done, i + 1)
                vec.tensor_tensor(vl[:, :], ps[:, V_BANK, :], vh[:, :], ALU.subtract).then_inc(vl_done, 1)
                taps_of(3, 1)
                dve.wait_ge(gate_read, i * 2 + 2)
                vec.scalar_tensor_tensor(out=y_tile(i), in0=tmp[:, :], scalar=1.0, in1=v_t[:, :],
                                         op0=ALU.add, op1=ALU.mult).then_inc(gate_done, 1)
                low(t + 5, 0, 0)
                taps_of(4, 0)
                low(t + 5, 0, 1)
                for j in range(NT):
                    dve.wait_ge(pth_done, i * NT + (j + 1))
                    c = slice(PT_AT[j], PT_AT[j + 1])
                    vec.tensor_tensor(ptl[:, c], ps[:, S0 + j, 0:PT_N[j]], pth[:, c], ALU.subtract).then_inc(ptl_done, 1)
                taps_of(4, 1)
                low(t + 6, 1, 0)
                low(t + 6, 1, 1)
                dve.wait_ge(pv_done, i + 1)
                dve.wait_ge(gate_done, i + 1)
                vec.tensor_tensor(y_tile(i), ps[:, O_BANK, :], y_tile(i), ALU.mult).then_inc(attn_done, 1)

            def forget():
                dve.wait_ge(f_act, 4)
                vec.scalar_tensor_tensor(out=fm, in0=fz, scalar=0.0, in1=fa, op0=ALU.min, op1=ALU.subtract) \
                   .then_inc(f_vec, 1)
                dve.wait_ge(f_vec, 1)
                vec.tensor_tensor_scan(fcum, one_row, fm, 0.0, ALU.mult, ALU.add).then_inc(f_vec, 1)
                dve.wait_ge(f_vec, 2)
                vec.tensor_scalar(fcum, fcum, 1.0 / SCALE, None, ALU.mult).then_inc(f_vec, 1)
                dve.wait_ge(f_act, 5)
                vec.tensor_tensor(cum4[:, SEQ:2 * SEQ].bitcast(F32R), fcum, cum4[:, 0:SEQ], ALU.subtract).then_inc(f_vec, 1)
                vec.tensor_scalar(cum4[:, 2 * SEQ:3 * SEQ], cum4[:, 0:SEQ], -1.0, None, ALU.mult).then_inc(f_vec, 1)
                dve.wait_ge(f_vec, 5)
                vec.tensor_scalar(cum4[:, 3 * SEQ:4 * SEQ], cum4[:, SEQ:2 * SEQ], -1.0, None, ALU.mult).then_inc(f_vec, 2)

            one_row = odd[0:HEADS, :]
            vec.memset(one_row, 1.0).then_inc(vec_const, 1)
            dve.wait_ge(vec_const, 7)

            body(0, True)
            with vec.Fori(1, HEADS) as i:
                body(i, False)

            def bias_z(j, par):
                if not isinstance(j, int) or j >= 2:
                    dve.wait_ge(z_read, j * 2 - 2)
                vec.tensor_copy(now_z[:, par:par + 1], col(hcols, GATE_C, j)).then_inc(nowz_done, 1)

            def gate(j, slot):
                dve.wait_ge(z_read, j * 2 + 2)
                vec.scalar_tensor_tensor(out=zbuf[:, slot, :], in0=tmp[:, :], scalar=1.0, in1=zbuf[:, slot, :],
                                         op0=ALU.add, op1=ALU.mult).then_inc(z_done, 1)

            def normed(j):
                dve.wait_ge(rstd_vec, 6)
                if not isinstance(j, int) or j:
                    dve.wait_ge(aff_done, j * 2)
                vec.tensor_copy(now_n[:, 0:1], hcn[:, ds(G_CN * HEADS + j, 1)]).then_inc(nown_done, 1)
                vec.tensor_copy(now_n[:, 1:2], hcn[:, ds(B_CN * HEADS + j, 1)]).then_inc(nown_done, 1)
                dve.wait_ge(nown_done, j * 2 + 2)
                vec.tensor_tensor(sq[:, 0, :], y_tile(HEADS + j), rstd[:, :], ALU.mult).then_inc(norm_done, 1)

            def gated(j, slot):
                dve.wait_ge(aff_done, j * 2 + 2)
                vec.scalar_tensor_tensor(out=y_tile(HEADS + j), in0=odd[:, :], scalar=1.0, in1=sq[:, 1, :],
                                         op0=ALU.add, op1=ALU.mult).then_inc(act_done, 1)
                dve.wait_ge(act_done, j + 1)
                dve.wait_ge(z_done, j + 1)
                vec.tensor_tensor(y_tile(HEADS + j), y_tile(HEADS + j), zbuf[:, slot, :], ALU.mult).then_inc(yc_done, 1)

            t, c = T_GATE, HEADS - 1
            for j in range(2):
                bias_z(j, (j + 1) % 2)
            glu(c)
            low(t + 1, 0, 0)
            conv(c, 0, 6)
            low(t + 1, 0, 1)
            conv(c, 6, 16)
            gate(0, 0)
            bias_z(2, 1)
            low(t + 2, 1, 0)
            conv(c, 16, 24)
            low(t + 2, 1, 1)
            conv(c, 24, TAPS)
            conv_end(c)
            gate(1, 1)
            bias_z(3, 0)
            low(t + 3, 0, 0)
            low(t + 3, 0, 1)
            vec.memset(sq_odd[:, :], 0.0).then_inc(sqo_done, 1)

            def center(j):
                vec.tensor_tensor(y_tile(HEADS + j), y_tile(HEADS + j), ps[:, V_BANK, :], ALU.subtract).then_inc(cent_done, 1)

            def add_square(j):
                dve.wait_ge(sq_done, j + 1)
                dve.wait_ge(sqo_done, (j - 1) // 2 + 1)
                vec.tensor_tensor(sq_odd[:, :], sq_odd[:, :], sq[:, j % 3, :], ALU.add).then_inc(sqo_done, 1)

            dve.wait_ge(mean_done, 1)
            for j in range(HEADS):
                center(j)
                if j >= 4 and j % 2 == 0:
                    add_square(j - 3)
                if j == 8:
                    gate(2, 2)
                    low(t + 4, 1, 0)
                    low(t + 4, 1, 1)
            add_square(HEADS - 3)
            add_square(HEADS - 1)
            dve.wait_ge(var_done, 1)
            vec.tensor_scalar(sq_odd[:, :], ps[:, O_BANK, :], LN_EPS, None, ALU.add).then_inc(rstd_vec, 1)
            dve.wait_ge(rstd_act, 2)
            vec.tensor_tensor(odd[:, :], rstd[:, :], rstd[:, :], ALU.mult).then_inc(rstd_vec, 1)
            dve.wait_ge(rstd_vec, 2)
            vec.tensor_tensor(odd[:, :], odd[:, :], sq_odd[:, :], ALU.mult).then_inc(rstd_vec, 1)
            dve.wait_ge(rstd_vec, 3)
            vec.tensor_scalar(odd[:, :], odd[:, :], -0.5, 1.5, ALU.mult, ALU.add).then_inc(rstd_vec, 1)
            dve.wait_ge(rstd_vec, 4)
            vec.tensor_tensor(rstd[:, :], rstd[:, :], odd[:, :], ALU.mult).then_inc(rstd_vec, 2)

            def gate_step(j, s):
                normed(j - 4)
                gate(j - 1, (s - 1) % 4)
                bias_z(j, (s + 1) % 2)
                low(j + (T_GATE + 1), s % 2, 0)
                gated(j - 4, s)
                low(j + (T_GATE + 1), s % 2, 1)

            with vec.Fori(1, HEADS // 4) as b:
                for s in range(4):
                    gate_step(b * 4 + s, s)

            def split_y(n, slot, src):
                dve.wait_ge(yh_done, n + 1)
                vec.tensor_tensor(yl[:, slot, :], src, yh[:, slot, :], ALU.subtract).then_inc(yl_done, 1)

            def out_pair(pair, m, s, nxt):
                t = pair + T_OUT
                split_y(pair * 2 + 1, 1, y_tile(m * 2 + 1))
                low(t + 1, s, 0)
                if nxt is not None:
                    split_y(pair * 2 + 2, 0, y_tile(nxt))
                low(t + 1, s, 1)

            split_y(0, 0, y_tile(0))
            gate(HEADS - 1, 3)
            out_pair(0, 0, 0, 2)
            for j in (HEADS - 4, HEADS - 3):
                normed(j)
                gated(j, j % 4)
            out_pair(1, 1, 1, 4)
            for j in (HEADS - 2, HEADS - 1):
                normed(j)
                gated(j, j % 4)
            with vec.Fori(1, OUT_PAIRS // 2 - 1) as b:
                for s in range(2):
                    out_pair(b * 2 + s, b * 2 + s, s, b * 4 + (2 * s + 2))
            out_pair(OUT_PAIRS - 2, OUT_PAIRS - 2, 0, 2 * OUT_PAIRS - 2)
            out_pair(OUT_PAIRS - 1, OUT_PAIRS - 1, 1, 0)

            def add_result(p, n):
                for g in range(2):
                    r = res[:, n, 1024 * p + SEQ * g:1024 * p + SEQ * (g + 1)]
                    vec.tensor_tensor(r, ps[:, (2 * n + g + 2) % 8, :], r, ALU.add).then_inc(evac_done, 1)

            dve.wait_ge(half_done, 2 * T_OUT + 2 * OUT_PAIRS)
            dve.wait_ge(res_ready, NT)
            for n in range(NT):
                add_result(0, n)
            with vec.Fori(0, OUT_PAIRS // 2 - 1) as b:
                for s in range(2):
                    out_pair(b * 2 + (OUT_PAIRS + s), b * 2 + s, s, b * 4 + (2 * s + 2))
            out_pair(N_OUT - 2, OUT_PAIRS - 2, 0, 2 * OUT_PAIRS - 2)
            split_y(2 * N_OUT - 1, 1, y_tile(2 * OUT_PAIRS - 1))

            dve.wait_ge(bcast_loaded, 48)
            for n in range(NT):
                dve.wait_ge(half_done, 2 * T_OUT + 2 * N_OUT - 2 + n + 1)
                add_result(1, n)
                dve.wait_ge(evac_done, 8 + 2 * n + 2)
                base = 12 * n
                for g in range(4):
                    vec.bn_stats(stats[:, g, :], res[:, n, SEQ * g:SEQ * (g + 1)]).then_inc(fin_vec, 1)
                dve.wait_ge(fin_vec, base + 4)
                vec.bn_aggr(mv[:, :], stats[:, :, :].rearrange("p a b -> p (a b)")).then_inc(fin_vec, 2)
                dve.wait_ge(fin_vec, base + 6)
                vec.tensor_scalar(mv[:, 1:2], mv[:, 1:2], LN_EPS, None, ALU.add).then_inc(fin_vec, 1)
                dve.wait_ge(fin_act, 4 * n + 2)
                vec.tensor_tensor(nt1[:, :], rs[:, :], rs[:, :], ALU.mult).then_inc(fin_vec, 1)
                dve.wait_ge(fin_vec, base + 8)
                vec.tensor_tensor(nt2[:, :], nt1[:, :], mv[:, 1:2], ALU.mult).then_inc(fin_vec, 1)
                dve.wait_ge(fin_vec, base + 9)
                vec.tensor_scalar(nt1[:, :], nt2[:, :], -0.5, 1.5, ALU.mult, ALU.add).then_inc(fin_vec, 1)
                dve.wait_ge(fin_vec, base + 10)
                vec.tensor_tensor(rs[:, :], rs[:, :], nt1[:, :], ALU.mult).then_inc(fin_vec, 1)
                dve.wait_ge(fin_vec, base + 11)
                vec.scalar_tensor_tensor(out=shift[:, :], in0=mv[:, 0:1], scalar=-1.0, in1=rs[:, :],
                                         op0=ALU.mult, op1=ALU.mult).then_inc(fin_vec, 1)
                for h in range(2):
                    dve.wait_ge(fin_act, 4 * n + 3 + h)
                    r, c = res[:, n, 1024 * h:1024 * (h + 1)], slice(1024 * h, 1024 * (h + 1))
                    vec.tensor_tensor(r, r, gpost_b[:, c], ALU.mult).then_inc(fin_pool, 1)
                    dve.wait_ge(fin_pool, 2 * n + h + 1)
                    vec.tensor_tensor(r, r, bpost_b[:, c], ALU.add).then_inc(row_done, 1)


_INS = ["x", "w_in", "b_in", "w_dw", "b_dw", "g_conv_norm", "b_conv_norm", "w_out", "b_out", "g_post", "b_post"]


def kernel(**inputs):
    import numpy as np
    import concourse.bacc as bacc
    from concourse.bass_utils import run_bass_kernel_spmd

    nc = bacc.Bacc("TRN2", target_bir_lowering=False, num_devices=1)
    arrays, args = {}, []
    for name in _INS:
        a = np.ascontiguousarray(inputs[name])
        arrays[f"in_{name}_dram"] = a
        args.append(nc.dram_tensor(f"in_{name}_dram", a.shape, mybir.dt.from_np(a.dtype), kind="ExternalInput").ap())
    out = nc.dram_tensor("out_0_dram", (1, SEQ, D), F32, kind="ExternalOutput").ap()
    scratch = nc.dram_tensor("forget_sums_dram", (HEADS, 4 * SEQ), F32).ap()
    build(nc, *args, out, scratch)
    r = run_bass_kernel_spmd(nc, [arrays], core_ids=[0])
    return r.results[0]["out_0_dram"]
```

```python
import math
from contextlib import ExitStack

import concourse.bass as bass
from concourse import mybir

F32 = mybir.dt.float32
F32R = mybir.dt.float32r
BF16 = mybir.dt.bfloat16
ACT = mybir.ActivationFunctionType
ALU = mybir.AluOpType
AX = mybir.AxisListType

P = 128
SEQ = 512
D = 2048
KT = D // P
HALF = KT // 2
NT = SEQ // P
HEADS = D // P
TAPS = 31
PAD = TAPS - 1
LN_EPS = 1e-5
ALPHA = 2.0 ** 0.25
SCALE = 1.0 / math.sqrt(P)
MASKED = -1e37

PER_HEAD = 6
T_BODY = 1
T_GATE = T_BODY + PER_HEAD * HEADS
T_OUT = T_GATE + HEADS
OUT_PAIRS = HEADS
N_OUT = 2 * OUT_PAIRS
FIN = 8
SLOTS = 4

VAL, GLU, GATE_C, Q, K, V, GATE_A = range(7)
F_COL = 6 * D
BODY_KINDS = (Q, K, V, GATE_A, VAL, GLU)
BODY_TAPS = (7, 7, 7, 6, 5, 0)
B_DW, G_CN, B_CN = range(3)
NOW = {Q: (0, False), K: (1, False), V: (2, False), GATE_A: (3, True), VAL: (4, True), GLU: (5, True)}

PT_N = [SEQ - P * j for j in range(NT)]
PT_AT = [sum(PT_N[:j]) for j in range(NT + 1)]
PR_AT = [P * i * (i + 1) // 2 for i in range(NT + 1)]


def col_of(kind, i):
    return (F_COL + HEADS if kind == GATE_A else kind * D) + P * i


def build(nc, x, w_in, b_in, w_dw, b_dw, g_cn, b_cn, w_out, b_out, g_post, b_post, out, scratch):
    ctx = ExitStack()
    with ctx:
        def sb(name, shape, dt=F32, where=ctx):
            return where.enter_context(nc.sbuf_tensor(name, shape, dt))

        def sem(name):
            return ctx.enter_context(nc.semaphore(name))

        y = sb("y", [P, 2 * HEADS, SEQ])
        y_flat = y[:, :, :].rearrange("p a b -> p (a b)")
        raw = sb("raw", [P, 2, HALF * P])
        wh = sb("wh", [P, SLOTS, HALF * P], F32R)
        wl = sb("wl", [P, SLOTS, HALF * P], F32R)
        u = sb("u", [P, PAD + SEQ])
        tmp = sb("tmp", [P, SEQ])
        odd = sb("odd", [P, SEQ])
        csum = sb("csum", [P, SEQ])
        ident = sb("ident", [P, P])
        ident16 = sb("ident16", [P, P], BF16)
        mask16 = sb("mask16", [P, P], BF16)
        mean_w = sb("mean_w", [P, P])
        cols = sb("cols", [P, 7 * HEADS])
        hcols = sb("hcols", [P, 7 * HEADS])
        cn = sb("cn", [P, 3 * HEADS])
        hcn = sb("hcn", [P, 3 * HEADS])
        taps = sb("taps", [P, HEADS, TAPS])
        now = sb("now", [P, 6])
        now_z = sb("now_z", [P, 2])
        now_n = sb("now_n", [P, 2])
        fbias = sb("fbias", [HEADS, 1])
        one = sb("one", [P, 1])
        row_max = sb("row_max", [P, NT])
        neg_max = sb("neg_max", [P, NT])
        row_sum = sb("row_sum", [P, NT])
        row_inv = sb("row_inv", [P, NT])
        stats = sb("stats", [P, NT, 4, 6])
        mv = sb("mv", [P, 2])
        var_eps = sb("var_eps", [P, 1])
        std = sb("std", [P, 1])
        rs = sb("rs", [P, 1])
        newton = sb("newton", [P, 1])

        first = ExitStack()
        parts = sb("parts", [P, 2 * PT_AT[NT]], F32R, first)
        v_t = sb("v_t", [P, SEQ], F32, first)
        vh = sb("vh", [P, NT * P], F32R, first)
        vl = sb("vl", [P, NT * P], F32R, first)
        probs = sb("probs", [P, PR_AT[NT]], F32, first)
        cum_q = sb("cum_q", [P, SEQ], F32R, first)
        cum_k = sb("cum_k", [P, SEQ], F32R, first)
        first.close()
        zbuf = sb("zbuf", [P, 4, SEQ])
        yh = sb("yh", [P, 2, SEQ], F32R)
        yl = sb("yl", [P, 2, SEQ], F32R)
        sq = sb("sq", [P, 3, SEQ])
        sq_odd = sb("sq_odd", [P, SEQ])
        rstd = sb("rstd", [P, SEQ])
        second = ExitStack()
        xh = sb("xh", [P, KT, SEQ], F32R, second)
        xl = sb("xl", [P, KT, SEQ], F32R, second)
        second.close()
        res = sb("res", [P, NT, D])
        bout_b = sb("bout_b", [P, D])
        gpost_b = sb("gpost_b", [P, D])
        bpost_b = sb("bpost_b", [P, D])
        yh_end = sb("yh_end", [P, 2, SEQ], F32R)
        yl_end = sb("yl_end", [P, 2, SEQ], F32R)

        ps = ctx.enter_context(nc.psum_tensor("ps", [P, 8, SEQ], F32))
        S0, V_BANK, O_BANK = 2, 6, 7
        qh, ql, kh, kl = (parts[:, SEQ * n:SEQ * (n + 1)] for n in range(4))
        pth, ptl = parts[:, 0:PT_AT[NT]], parts[:, PT_AT[NT]:]
        x_rows = y_flat[:, 0:NT * D].rearrange("p (t d) -> p t d", t=NT)
        rows = y_flat[:, NT * D:]
        cum4 = y_flat[0:HEADS, 12 * SEQ:16 * SEQ]
        fz, fa = probs[0:HEADS, 0:SEQ], probs[0:HEADS, SEQ:2 * SEQ]
        fm, fcum = v_t[0:HEADS, :], tmp[0:HEADS, :]

        x_loaded = [sem(f"x_loaded{c}") for c in range(4)]
        rows_loaded, bcast_loaded, stored = sem("rows_loaded"), sem("bcast_loaded"), sem("stored")
        raw_full = [sem("raw_full0"), sem("raw_full1")]
        cum_stored, cum_loaded = sem("cum_stored"), sem("cum_loaded")
        res_loaded = sem("res_loaded")
        const_done, vec_const = sem("const_done"), sem("vec_const")
        xt_turned, xh_done, xl_done = sem("xt_turned"), sem("xh_done"), sem("xl_done")
        cols_turned, cols_done = sem("cols_turned"), sem("cols_done")
        high_done, low_done, half_done = sem("high_done"), sem("low_done"), sem("half_done")
        f_act, f_vec = sem("f_act"), sem("f_vec")
        qk_high, qk_low = sem("qk_high"), sem("qk_low")
        vt_done, v_turned, vh_done, vl_done = sem("vt_done"), sem("v_turned"), sem("vh_done"), sem("vl_done")
        scores_done, max_done, negmax_done = sem("scores_done"), sem("max_done"), sem("negmax_done")
        exp_done, inv_done, probs_done = sem("exp_done"), sem("inv_done"), sem("probs_done")
        p_turned, pth_done, ptl_done, pv_done = sem("p_turned"), sem("pth_done"), sem("ptl_done"), sem("pv_done")
        now_done, nowz_done, nown_done = sem("now_done"), sem("nowz_done"), sem("nown_done")
        gate_read, gate_done, attn_done = sem("gate_read"), sem("gate_done"), sem("attn_done")
        val_read, glu_tanh, u_done, tap_done = sem("val_read"), sem("glu_tanh"), sem("u_done"), sem("tap_done")
        conv_done, csum_done, mean_done = sem("conv_done"), sem("csum_done"), sem("mean_done")
        cent_done, sq_done, sqe_done, sqo_done = sem("cent_done"), sem("sq_done"), sem("sqe_done"), sem("sqo_done")
        var_done, rstd_act, rstd_vec = sem("var_done"), sem("rstd_act"), sem("rstd_vec")
        z_read, z_done = sem("z_read"), sem("z_done")
        norm_done, aff_done, act_done, yc_done = sem("norm_done"), sem("aff_done"), sem("act_done"), sem("yc_done")
        yh_done, yl_done = sem("yh_done"), sem("yl_done")
        res_scaled, res_ready, evac_done = sem("res_scaled"), sem("res_ready"), sem("evac_done")
        fin_vec, fin_act, row_done = sem("fin_vec"), sem("fin_act"), sem("row_done")
        sum_done = sem("sum_done")
        stats_done, scaled_done = sem("stats_done"), sem("scaled_done")

        block = ctx.enter_context(nc.Block())

        def ds(i, n):
            return bass.ds(i, n)

        @block.sync
        def _(sp):
            def load_in(t, col, second_first=False):
                for h in (1, 0) if second_first else (0, 1):
                    if not (second_first and h == 0):
                        sp.wait_ge(low_done, 2 * t + h - 1)
                    src = w_in[D // 2 * h:D // 2 * (h + 1), ds(col, P)]
                    sp.dma_start(raw[:, h, :].rearrange("p (k c) -> p k c", k=HALF),
                                 src.rearrange("(k p) c -> p k c", p=P)).then_inc(raw_full[h], 16)

            def load_out(t, row, half_cols):
                for h in range(2):
                    sp.wait_ge(low_done, 2 * t + h - 1)
                    sp.dma_start(raw[:, h, :], w_out[ds(row + P * h, P), half_cols * 1024:half_cols * 1024 + 1024]) \
                      .then_inc(raw_full[h], 16)

            def load_cum(h):
                sp.dma_start(cum_q[0:2, :].bitcast(F32),
                             scratch[ds(h, 1), 0:2 * SEQ].rearrange("a (r n) -> (a r) n", r=2)).then_inc(cum_loaded, 16)
                sp.dma_start(cum_k[2:4, :].bitcast(F32),
                             scratch[ds(h, 1), 2 * SEQ:4 * SEQ].rearrange("a (r n) -> (a r) n", r=2)).then_inc(cum_loaded, 16)

            def load_first(h):
                src = w_in[D // 2 * h:D // 2 * (h + 1), F_COL:F_COL + P]
                sp.dma_start(raw[:, h, :].rearrange("p (k c) -> p k c", k=HALF),
                             src.rearrange("(k p) c -> p k c", p=P)).then_inc(raw_full[h], 16)

            x_v = x.rearrange("a (t p) d -> p (a t) d", p=P)
            for c in range(4):
                sp.dma_start(x_rows[:, :, SEQ * c:SEQ * (c + 1)], x_v[:, :, SEQ * c:SEQ * (c + 1)]) \
                  .then_inc(x_loaded[c], 16)
                if c == 1:
                    load_first(0)
            load_first(1)
            sp.dma_start(rows[0:TAPS, 0:D], w_dw).then_inc(rows_loaded, 16)
            sp.dma_start(rows[0:6 * HEADS, D:D + P], b_in[0:6 * D].rearrange("(j p) -> j p", p=P)).then_inc(rows_loaded, 16)
            sp.dma_start(rows[6 * HEADS:7 * HEADS, D:D + P],
                         b_in[F_COL + HEADS:F_COL + HEADS + D].rearrange("(j p) -> j p", p=P)).then_inc(rows_loaded, 16)
            for n, vec in enumerate((b_dw, g_cn, b_cn)):
                sp.dma_start(rows[n * HEADS:(n + 1) * HEADS, D + P:D + 2 * P],
                             vec.rearrange("(j p) -> j p", p=P)).then_inc(rows_loaded, 16)
            sp.dma_start(fbias[:, :], b_in[F_COL:F_COL + HEADS].rearrange("(j p) -> j p", p=1)).then_inc(rows_loaded, 16)
            load_in(1, col_of(Q, 0))

            def body(i):
                for s, kind in enumerate(BODY_KINDS):
                    t = i * PER_HEAD + (T_BODY + s)
                    if s + 1 < PER_HEAD:
                        load_in(t + 1, col_of(BODY_KINDS[s + 1], 0) + i * P, BODY_KINDS[s + 1] == VAL)
                    if s == 1 and isinstance(i, int):
                        sp.wait_ge(f_vec, 7)
                        sp.dma_start(scratch, cum4).then_inc(cum_stored, 16)
                        sp.wait_ge(cum_stored, 16)
                        sp.wait_ge(const_done, 8)
                        load_cum(0)

            def next_cum(i):
                sp.wait_ge(scores_done, i * NT + NT)
                load_cum(i + 1)

            body(0)
            next_cum(0)
            load_in(T_BODY + PER_HEAD, col_of(Q, 1))
            with nc.sync.Fori(1, HEADS - 1) as i:
                body(i)
                next_cum(i)
                load_in(i * PER_HEAD + (T_BODY + PER_HEAD), col_of(Q, 1) + i * P)
            i = HEADS - 1
            for s in range(1, PER_HEAD):
                load_in(T_BODY + i * PER_HEAD + s, col_of(BODY_KINDS[s], i))
            with nc.sync.Fori(0, HEADS) as j:
                load_in(j + T_GATE, col_of(GATE_C, 0) + j * P)
            for p in range(2):
                t = T_OUT + p * OUT_PAIRS
                with nc.sync.Fori(0, OUT_PAIRS // 2) as m:
                    load_out(m + t, D + m * (2 * P), p)
                with nc.sync.Fori(0, OUT_PAIRS // 2) as m:
                    load_out(m + (t + OUT_PAIRS // 2), m * (2 * P), p)
            for t in range(NT):
                for h in range(2):
                    c = slice(1024 * h, 1024 * (h + 1))
                    sp.wait_ge(row_done, 2 * t + h + 1)
                    sp.dma_start(out[0, P * t:P * (t + 1), c], res[:, t, c]).then_inc(stored, 16)
            sp.wait_ge(stored, 32 * NT)

        @block.gpsimd
        def _(pool):
            nc.gpsimd.memset(ident[:, :], 0.0).then_inc(const_done, 1)
            nc.gpsimd.memset(ident16[:, :], 0.0).then_inc(const_done, 1)
            nc.gpsimd.memset(mask16[:, :], 0.0).then_inc(const_done, 1)
            pool.wait_ge(const_done, 3)
            nc.gpsimd.affine_select(out=ident[:, :], in_=ident[:, :], compare_op=ALU.not_equal, fill=1.0,
                                    base=0, pattern=[[-1, P]], channel_multiplier=1).then_inc(const_done, 1)
            nc.gpsimd.affine_select(out=ident16[:, :], in_=ident16[:, :], compare_op=ALU.not_equal, fill=1.0,
                                    base=0, pattern=[[-1, P]], channel_multiplier=1).then_inc(const_done, 1)
            nc.gpsimd.affine_select(out=mask16[:, :], in_=mask16[:, :], compare_op=ALU.is_ge, fill=MASKED,
                                    base=0, pattern=[[-1, P]], channel_multiplier=1).then_inc(const_done, 1)
            pool.wait_ge(vec_const, 4)
            nc.gpsimd.memset(cum_q[0:4, :].bitcast(F32), 1.0).then_inc(const_done, 1)
            nc.gpsimd.memset(cum_k[0:4, :].bitcast(F32), 1.0).then_inc(const_done, 1)

            pool.wait_ge(vec_const, 6)

            pool.wait_ge(conv_done, 1)
            nc.gpsimd.tensor_tensor(csum[:, :], csum[:, :], y[:, HEADS, :], ALU.add).then_inc(csum_done, 1)
            with nc.gpsimd.Fori(1, HEADS) as i:
                pool.wait_ge(conv_done, i + 1)
                pool.wait_ge(csum_done, i)
                nc.gpsimd.tensor_tensor(csum[:, :], csum[:, :], y[:, ds(HEADS + i, 1), :].rearrange("p a b -> p (a b)"),
                                        ALU.add).then_inc(csum_done, 1)
            pool.wait_ge(mean_done, 1)
            nc.gpsimd.memset(csum[:, :], 0.0).then_inc(sqe_done, 1)
            for j in range(0, HEADS, 2):
                pool.wait_ge(sq_done, j + 1)
                pool.wait_ge(sqe_done, j // 2 + 1)
                nc.gpsimd.tensor_tensor(csum[:, :], csum[:, :], sq[:, j % 3, :], ALU.add).then_inc(sqe_done, 1)

            def repeat_row(step, dst, src):
                pool.wait_ge(half_done, 2 * T_OUT + step)
                with nc.allow_non_contiguous_dma(reason="a row repeated over the partitions"):
                    nc.gpsimd.dma_start(dst[:, :], src.partition_broadcast(P)).then_inc(bcast_loaded, 16)

            repeat_row(1, bout_b, b_out)
            for t in range(NT):
                pool.wait_ge(half_done, 2 * T_OUT + 4 * (t + 1))
                nc.gpsimd.dma_start(res[:, t, :], x[0, P * t:P * (t + 1), :]).then_inc(res_loaded, 16)
                pool.wait_ge(res_loaded, 16 * (t + 1))
                nc.gpsimd.tensor_scalar(res[:, t, :], res[:, t, :], ALPHA, None, ALU.mult).then_inc(res_scaled, 1)
                pool.wait_ge(res_scaled, t + 1)
                if t == 0:
                    pool.wait_ge(bcast_loaded, 16)
                nc.gpsimd.tensor_tensor(res[:, t, :], res[:, t, :], bout_b[:, :], ALU.add).then_inc(res_ready, 1)
            repeat_row(24, gpost_b, g_post)
            repeat_row(28, bpost_b, b_post)

        @block.scalar
        def _(act):
            def high(t, par, h, lag=4):
                act.wait_ge(raw_full[h], 16 * (t + 1))
                if not isinstance(t, int) or t >= 2:
                    act.wait_ge(half_done, 2 * t + (h + 1 - lag))
                nc.scalar.activation(wh[:, 2 * par + h, :], raw[:, h, :], ACT.Copy).then_inc(high_done, 1)

            def bank_of(par):
                return ps[:, par, :]

            def bias_of(kind):
                return now[:, NOW[kind][0]:NOW[kind][0] + 1]

            def tile_done(t):
                act.wait_ge(half_done, 2 * t + 2)

            def x_high(kt):
                act.wait_ge(xt_turned, kt + 1)
                nc.scalar.activation(xh[:, kt, :], ps[:, S0 + kt % 4, :], ACT.Copy).then_inc(xh_done, 1)

            for kt in range(HALF):
                x_high(kt)
            high(0, 0, 0)
            for kt in range(HALF, KT):
                x_high(kt)
            high(0, 0, 1)
            high(1, 1, 0)
            high(1, 1, 1)
            act.wait_ge(cols_turned, 1)
            nc.scalar.activation(cols[:, :], ps[:, V_BANK, 0:7 * HEADS], ACT.Copy).then_inc(cols_done, 1)
            nc.scalar.activation(hcols[:, :], ps[:, V_BANK, 0:7 * HEADS], ACT.Copy, scale=0.5).then_inc(cols_done, 1)
            nc.scalar.activation(cn[:, :], ps[:, V_BANK, 128:128 + 3 * HEADS], ACT.Copy).then_inc(cols_done, 1)
            nc.scalar.activation(hcn[:, :], ps[:, V_BANK, 128:128 + 3 * HEADS], ACT.Copy, scale=0.5).then_inc(cols_done, 1)
            act.wait_ge(cols_turned, 2)
            nc.scalar.activation(taps[:, :, :].rearrange("p a b -> p (a b)"), ps[:, O_BANK, 0:HEADS * TAPS],
                                 ACT.Copy).then_inc(cols_done, 1)
            act.wait_ge(cols_done, 5)

            tile_done(0)
            act.wait_ge(rows_loaded, 16 * 7)
            act.wait_ge(vec_const, 6)
            nc.scalar.activation(fz, ps[0:HEADS, 0, :], ACT.Identity, bias=fbias[:, :]).then_inc(f_act, 1)
            nc.scalar.activation(fa, ps[0:HEADS, 0, :], ACT.Abs, bias=fbias[:, :]).then_inc(f_act, 1)
            act.wait_ge(f_act, 2)
            nc.scalar.activation(fa, fa, ACT.Exp, scale=-1.0).then_inc(f_act, 1)
            act.wait_ge(f_act, 3)
            nc.scalar.activation(fa, fa, ACT.Ln, bias=one[0:HEADS, :]).then_inc(f_act, 1)
            act.wait_ge(f_vec, 3)
            nc.scalar.activation(cum4[:, 0:SEQ].bitcast(F32R), fcum, ACT.Copy).then_inc(f_act, 1)

            def glu_gate(t, i):
                tile_done(t)
                act.wait_ge(gate_done, i + 1)
                nc.scalar.activation(tmp[:, :], bank_of(0), ACT.Tanh, bias=bias_of(GLU), scale=0.5) \
                  .then_inc(glu_tanh, 1)

            def body(i, i0):
                t = i * PER_HEAD + T_BODY
                if not i0:
                    glu_gate(t - 1, i - 1)
                high(t + 1, 0, 0)
                high(t + 1, 0, 1)
                tile_done(t)
                if not i0:
                    act.wait_ge(pv_done, i)
                act.wait_ge(now_done, i + 1)
                nc.scalar.activation(qh, bank_of(1), ACT.Identity, bias=bias_of(Q)).then_inc(qk_high, 1)
                high(t + 2, 1, 0)
                high(t + 2, 1, 1)
                tile_done(t + 1)
                nc.scalar.activation(kh, bank_of(0), ACT.Identity, bias=bias_of(K)).then_inc(qk_high, 1)
                high(t + 3, 0, 0)
                high(t + 3, 0, 1)
                act.wait_ge(negmax_done, i + 1)
                for b in range(NT):
                    nc.scalar.activation(probs[:, PR_AT[b]:PR_AT[b + 1]], ps[:, S0 + b, 0:P * (b + 1)], ACT.Exp,
                                         bias=neg_max[:, b:b + 1], scale=SCALE,
                                         accum_out=row_sum[:, b:b + 1]).then_inc(exp_done, 1)
                tile_done(t + 2)
                nc.scalar.activation(v_t[:, :], bank_of(1), ACT.Identity, bias=bias_of(V)).then_inc(vt_done, 1)
                high(t + 4, 1, 0)
                high(t + 4, 1, 1)
                act.wait_ge(v_turned, i + 1)
                nc.scalar.activation(vh[:, :], ps[:, V_BANK, :], ACT.Copy).then_inc(vh_done, 1)
                tile_done(t + 3)
                nc.scalar.activation(v_t[:, :], bank_of(0), ACT.Identity,
                                     bias=bias_of(GATE_A), scale=0.5).then_inc(gate_read, 1)
                if not i0:
                    act.wait_ge(u_done, i)
                nc.scalar.activation(tmp[:, :], bank_of(0), ACT.Tanh, bias=bias_of(GATE_A), scale=0.5) \
                  .then_inc(gate_read, 1)
                high(t + 5, 0, 0)
                high(t + 5, 0, 1)
                for j in range(NT):
                    act.wait_ge(p_turned, i * NT + (j + 1))
                    nc.scalar.activation(pth[:, PT_AT[j]:PT_AT[j + 1]], ps[:, S0 + j, 0:PT_N[j]], ACT.Copy) \
                      .then_inc(pth_done, 1)
                tile_done(t + 4)
                if not i0:
                    act.wait_ge(conv_done, i)
                act.wait_ge(vec_const, 6)
                nc.scalar.activation(u[:, PAD:], bank_of(1), ACT.Identity, bias=bias_of(VAL), scale=0.5) \
                  .then_inc(val_read, 1)
                high(t + 6, 1, 0)
                high(t + 6, 1, 1)

            body(0, True)
            with nc.scalar.Fori(1, HEADS) as i:
                body(i, False)

            def gate_c(t, j, slot, par):
                tile_done(t)
                act.wait_ge(attn_done, HEADS)
                act.wait_ge(nowz_done, j + 1)
                if not isinstance(j, int) or j >= 4:
                    act.wait_ge(yc_done, j - 3)
                nc.scalar.activation(zbuf[:, slot, :], bank_of(par), ACT.Identity,
                                     bias=now_z[:, par:par + 1], scale=0.5).then_inc(z_read, 1)
                if isinstance(j, int) and j == 0:
                    act.wait_ge(u_done, HEADS)
                else:
                    act.wait_ge(z_done, j)
                nc.scalar.activation(tmp[:, :], bank_of(par), ACT.Tanh,
                                     bias=now_z[:, par:par + 1], scale=0.5).then_inc(z_read, 1)

            def finish_conv(j, slot):
                act.wait_ge(norm_done, j + 1)
                if not isinstance(j, int) or j:
                    act.wait_ge(act_done, j)
                nc.scalar.activation(odd[:, :], sq[:, 0, :], ACT.Tanh, bias=now_n[:, 1:2], scale=now_n[:, 0:1]) \
                  .then_inc(aff_done, 1)
                nc.scalar.activation(sq[:, 1, :], sq[:, 0, :], ACT.Identity, bias=now_n[:, 1:2],
                                     scale=now_n[:, 0:1]).then_inc(aff_done, 1)

            t = T_GATE
            glu_gate(t - 1, HEADS - 1)
            high(t + 1, 0, 0)
            high(t + 1, 0, 1)
            gate_c(t, 0, 0, 1)
            high(t + 2, 1, 0)
            high(t + 2, 1, 1)
            gate_c(t + 1, 1, 1, 0)
            high(t + 3, 0, 0)
            high(t + 3, 0, 1)
            for j in range(HEADS):
                act.wait_ge(cent_done, j + 1)
                if j >= 3:
                    act.wait_ge(sqo_done if j % 2 == 0 else sqe_done, (j - 3) // 2 + 2)
                nc.scalar.activation(sq[:, j % 3, :], y[:, HEADS + j, :], ACT.Square).then_inc(sq_done, 1)
                if j == 7:
                    gate_c(t + 2, 2, 2, 1)
                    high(t + 4, 1, 0)
                    high(t + 4, 1, 1)
            def root():
                act.wait_ge(rstd_vec, 1)
                nc.scalar.activation(odd[:, :], sq_odd[:, :], ACT.Ln).then_inc(rstd_act, 1)
                act.wait_ge(rstd_act, 1)
                nc.scalar.activation(rstd[:, :], odd[:, :], ACT.Exp, scale=-0.5).then_inc(rstd_act, 1)

            def gate_step(j, s):
                gate_c(j + (T_GATE - 1), j - 1, (s - 1) % 4, s % 2)
                high(j + (T_GATE + 1), s % 2, 0)
                if isinstance(j, int) and j == 4:
                    high(j + (T_GATE + 1), s % 2, 1)
                    root()
                    finish_conv(j - 4, s)
                else:
                    finish_conv(j - 4, s)
                    high(j + (T_GATE + 1), s % 2, 1)

            for j in range(4, 8):
                gate_step(j, j % 4)
            with nc.scalar.Fori(2, HEADS // 4) as b:
                for s in range(4):
                    gate_step(b * 4 + s, s)

            def y_tile(k):
                return y[:, ds(k, 1), :].rearrange("p a b -> p (a b)")

            def split_y(slot, src):
                nc.scalar.activation(yh[:, slot, :], src, ACT.Copy).then_inc(yh_done, 1)

            def out_pair(pair, m, s, nxt, conv_tile=None):
                t = pair + T_OUT
                high(t + 1, s, 0, lag=3)
                split_y(1, y_tile(m * 2 + 1))
                if conv_tile is not None:
                    finish_conv(conv_tile, conv_tile % 4)
                high(t + 1, s, 1, lag=3)
                split_y(0, y_tile(nxt))

            act.wait_ge(attn_done, HEADS)
            split_y(0, y_tile(0))
            gate_c(T_OUT - 1, HEADS - 1, 3, 0)
            for m in range(4):
                out_pair(m, m, m % 2, 2 * m + 2, HEADS - 4 + m)
            with nc.scalar.Fori(2, OUT_PAIRS // 4) as b:
                for s in range(2):
                    out_pair(b * 2 + s, b * 2 + s, s, b * 4 + (2 * s + 2))
            act.wait_ge(yc_done, HEADS)
            with nc.scalar.Fori(OUT_PAIRS // 4, OUT_PAIRS // 2 - 1) as b:
                for s in range(2):
                    out_pair(b * 2 + s, b * 2 + s, s, b * 4 + (2 * s + 2))
            out_pair(OUT_PAIRS - 2, OUT_PAIRS - 2, 0, 2 * OUT_PAIRS - 2)
            out_pair(OUT_PAIRS - 1, OUT_PAIRS - 1, 1, 0)
            with nc.scalar.Fori(0, OUT_PAIRS // 2 - 1) as b:
                for s in range(2):
                    out_pair(b * 2 + (OUT_PAIRS + s), b * 2 + s, s, b * 4 + (2 * s + 2))
            t = T_OUT + N_OUT - 2
            high(t + 1, 0, 0, lag=3)
            split_y(1, y_tile(2 * OUT_PAIRS - 3))
            high(t + 1, 0, 1)
            for n in range(2):
                nc.scalar.activation(yh_end[:, n, :], y_tile(2 * OUT_PAIRS - 2 + n), ACT.Copy).then_inc(yh_done, 1)

            for n in range(NT):
                act.wait_ge(fin_vec, FIN * n + 4)
                nc.scalar.activation(std[:, :], var_eps[:, :], ACT.Sqrt).then_inc(fin_act, 1)

        @block.tensor
        def _(pe):
            def mm3(o, ah, al, bh, bl, start):
                nc.tensor.matmul(o, ah, bh, start=start, stop=False, skip_group_check=True)
                nc.tensor.matmul(o, ah, bl, start=False, stop=False, skip_group_check=True)
                return nc.tensor.matmul(o, al, bh, start=False, stop=True, skip_group_check=True)

            def half(t, par, h, beside=None):
                pe.wait_ge(low_done, 2 * t + (h + 1))
                for k in range(HALF):
                    if beside is not None:
                        beside(k)
                    a = slice(P * k, P * (k + 1))
                    last = mm3(ps[:, par, :], wh[:, 2 * par + h, a], wl[:, 2 * par + h, a],
                               xh[:, HALF * h + k, :], xl[:, HALF * h + k, :], h == 0 and k == 0)
                last.then_inc(half_done, 1)

            pe.wait_ge(const_done, 6)
            def turn_x(kt):
                if kt % 4 == 0:
                    pe.wait_ge(x_loaded[kt // 4], 16)
                if kt >= 4:
                    pe.wait_ge(xl_done, kt - 3)
                for n in range(NT):
                    last = nc.tensor.transpose(ps[:, S0 + kt % 4, P * n:P * (n + 1)],
                                               x_rows[:, n, P * kt:P * (kt + 1)], ident[:, :])
                last.then_inc(xt_turned, 1)

            for kt in range(HALF):
                turn_x(kt)
            pe.wait_ge(xl_done, HALF)
            half(0, 0, 0, lambda k: turn_x(HALF + k))
            pe.wait_ge(xl_done, KT)
            half(0, 0, 1)
            pe.wait_ge(rows_loaded, 16 * 7)
            nc.tensor.transpose(ps[:, V_BANK, 0:7 * HEADS], rows[0:7 * HEADS, D:D + P], ident[0:7 * HEADS, 0:7 * HEADS])
            nc.tensor.transpose(ps[:, V_BANK, 128:128 + 3 * HEADS], rows[0:3 * HEADS, D + P:D + 2 * P],
                                ident[0:3 * HEADS, 0:3 * HEADS]).then_inc(cols_turned, 1)
            for c in range(HEADS):
                last = nc.tensor.transpose(ps[:, O_BANK, TAPS * c:TAPS * (c + 1)], rows[0:TAPS, P * c:P * (c + 1)],
                                           ident[0:TAPS, 0:TAPS])
            last.then_inc(cols_turned, 1)

            def body(i, i0):
                t = i * PER_HEAD + T_BODY
                if not i0:
                    pe.wait_ge(val_read, i)
                half(t, 1, 0)
                half(t, 1, 1)
                if i0:
                    pe.wait_ge(f_act, 2)
                else:
                    pe.wait_ge(glu_tanh, i)
                half(t + 1, 0, 0)
                half(t + 1, 0, 1)
                pe.wait_ge(qk_low, i * 2 + 1)
                half(t + 2, 1, 0)
                pe.wait_ge(qk_low, i * 2 + 2)
                pe.wait_ge(cum_loaded, i * 32 + 32)
                if not i0:
                    pe.wait_ge(ptl_done, i * NT)
                for b in range(NT):
                    o, m, c = ps[:, S0 + b, 0:P * (b + 1)], slice(P * b, P * (b + 1)), slice(0, P * (b + 1))
                    nc.tensor.matmul(o, cum_q[:, m], cum_k[:, c], start=True, stop=False, skip_group_check=True)
                    nc.tensor.matmul(ps[:, S0 + b, m], ident16[:, :], mask16[:, :], start=False, stop=False,
                                     skip_group_check=True)
                    mm3(o, qh[:, m], ql[:, m], kh[:, c], kl[:, c], False).then_inc(scores_done, 1)
                half(t + 2, 1, 1)
                half(t + 3, 0, 0)
                pe.wait_ge(vt_done, i + 1)
                if not i0:
                    pe.wait_ge(vl_done, i)
                for b in range(NT):
                    last = nc.tensor.transpose(ps[:, V_BANK, P * b:P * (b + 1)], v_t[:, P * b:P * (b + 1)], ident[:, :])
                last.then_inc(v_turned, 1)
                half(t + 3, 0, 1)
                half(t + 4, 1, 0)
                pe.wait_ge(probs_done, i * NT + NT)
                for j in range(NT):
                    for b in range(j, NT):
                        last = nc.tensor.transpose(ps[:, S0 + j, P * (b - j):P * (b - j + 1)],
                                                   probs[:, PR_AT[b] + P * j:PR_AT[b] + P * (j + 1)], ident[:, :])
                    last.then_inc(p_turned, 1)
                half(t + 4, 1, 1)
                pe.wait_ge(gate_read, i * 2 + 2)
                half(t + 5, 0, 0)
                pe.wait_ge(ptl_done, i * NT + NT)
                pe.wait_ge(vl_done, i + 1)
                if not i0:
                    pe.wait_ge(attn_done, i)
                for j in range(NT):
                    a, c = slice(P * j, P * (j + 1)), slice(PT_AT[j], PT_AT[j + 1])
                    last = mm3(ps[:, O_BANK, P * j:SEQ], vh[:, a], vl[:, a], pth[:, c], ptl[:, c], j == 0)
                last.then_inc(pv_done, 1)
                half(t + 5, 0, 1)

            body(0, True)
            with nc.tensor.Fori(1, HEADS) as i:
                body(i, False)

            for j in range(4):
                if j == 0:
                    pe.wait_ge(val_read, HEADS)
                elif j == 1:
                    pe.wait_ge(glu_tanh, HEADS)
                else:
                    pe.wait_ge(z_read, 2 * j - 2)
                half(T_GATE + j, (j + 1) % 2, 0)
                half(T_GATE + j, (j + 1) % 2, 1)
                if j == 2:
                    pe.wait_ge(csum_done, HEADS)
                    pe.wait_ge(vl_done, HEADS)
                    nc.tensor.matmul(ps[:, V_BANK, :], mean_w[:, :], csum[:, :], start=True, stop=True) \
                      .then_inc(mean_done, 1)
            pe.wait_ge(z_read, 6)
            half(T_GATE + 4, 1, 0)
            pe.wait_ge(sqe_done, HEADS // 2 + 1)
            pe.wait_ge(sqo_done, HEADS // 2 + 1)
            pe.wait_ge(attn_done, HEADS)
            nc.tensor.matmul(ps[:, O_BANK, :], mean_w[:, :], csum[:, :], start=True, stop=False)
            nc.tensor.matmul(ps[:, O_BANK, :], mean_w[:, :], sq_odd[:, :], start=False, stop=True).then_inc(var_done, 1)
            half(T_GATE + 4, 1, 1)
            for j in range(5, 8):
                pe.wait_ge(z_read, 2 * j - 2)
                half(T_GATE + j, (j + 1) % 2, 0)
                half(T_GATE + j, (j + 1) % 2, 1)
            with nc.tensor.Fori(2, HEADS // 4) as b:
                for s in range(4):
                    pe.wait_ge(z_read, b * 8 + (2 * s - 2))
                    half(b * 4 + (T_GATE + s), (s + 1) % 2, 0)
                    half(b * 4 + (T_GATE + s), (s + 1) % 2, 1)

            def bank(n, g):
                return (2 * n + g + 2) % 8

            def ready(step):
                pe.wait_ge(low_done, step + (2 * T_OUT + 1))
                pe.wait_ge(yl_done, step + 1)

            def slot_of(q):
                return (2 * T_OUT + q) % SLOTS

            def step_mm(step, q, tokens=range(NT), begin=False, own_y=True):
                for n in tokens:
                    for g in range(2):
                        a, c = slice(P * n, P * (n + 1)), slice(SEQ * g, SEQ * (g + 1))
                        at_end = q >= 2 and len(tokens) == 1 and own_y
                        high_y, low_y = (yh_end, yl_end) if at_end else (yh, yl)
                        last = mm3(ps[:, bank(n, g), :], high_y[:, q % 2, a], low_y[:, q % 2, a],
                                   wh[:, slot_of(q), c], wl[:, slot_of(q), c], begin)
                return last

            per_pass = 2 * OUT_PAIRS
            for p in range(2):
                at = p * per_pass
                ready(at)
                if p == 0:
                    pe.wait_ge(rstd_vec, 2)
                    pe.wait_ge(cent_done, HEADS)
                    pe.wait_ge(ptl_done, HEADS * NT)
                for n in range(NT):
                    for g in range(2):
                        if p == 0 and bank(n, g) < 2:
                            pe.wait_ge(z_read, 2 * HEADS)
                        if p == 1:
                            pe.wait_ge(evac_done, 2 * n + g + 1)
                        a, c = slice(P * n, P * (n + 1)), slice(SEQ * g, SEQ * (g + 1))
                        last = mm3(ps[:, bank(n, g), :], yh[:, 0, a], yl[:, 0, a],
                                   wh[:, slot_of(0), c], wl[:, slot_of(0), c], True)
                last.then_inc(half_done, 1)
                for q in range(1, 4):
                    ready(at + q)
                    step_mm(at + q, q).then_inc(half_done, 1)
                with nc.tensor.Fori(1, OUT_PAIRS // 2 - 1) as b:
                    for q in range(4):
                        ready(b * 4 + (at + q))
                        step_mm(b * 4 + (at + q), q).then_inc(half_done, 1)
                if p == 0:
                    for q in range(3):
                        ready(at + per_pass - 4 + q)
                        step_mm(at + per_pass - 4 + q, q).then_inc(half_done, 1)
                    ready(at + per_pass - 1)
                    for n in range(NT):
                        last = step_mm(at + per_pass - 1, 3, [n], own_y=False)
                        last.then_inc(sum_done if n < NT - 1 else half_done, 1)
            at = 2 * per_pass - 4
            for n, qs in ((0, (0, 1)), (1, (0, 1)), (0, (2, 3)), (1, (2, 3)), (2, (0, 1, 2, 3)), (3, (0, 1, 2, 3))):
                for q in qs:
                    if n == 0:
                        ready(at + q)
                    last = step_mm(at + q, q, [n])
                if qs[-1] == 3:
                    last.then_inc(half_done, 1)

        @block.vector
        def _(dve):
            vec = nc.vector

            def low(t, par, h):
                dve.wait_ge(high_done, 2 * t + (h + 1))
                vec.tensor_tensor(wl[:, 2 * par + h, :], raw[:, h, :], wh[:, 2 * par + h, :], ALU.subtract) \
                   .then_inc(low_done, 1)

            def col(table, kind, i):
                return table[:, ds(kind * HEADS + i, 1)]

            def y_tile(k):
                return y[:, ds(k, 1), :].rearrange("p a b -> p (a b)")

            vec.memset(mean_w[:, :], 1.0 / D).then_inc(vec_const, 1)
            vec.memset(one[:, :], 1.0).then_inc(vec_const, 1)
            vec.memset(cum_q[:, :].bitcast(F32), 0.0).then_inc(vec_const, 1)
            vec.memset(cum_k[:, :].bitcast(F32), 0.0).then_inc(vec_const, 1)
            vec.memset(u[:, 0:PAD], 0.0).then_inc(vec_const, 1)
            vec.memset(csum[:, :], 0.0).then_inc(vec_const, 1)

            def x_low(kt):
                dve.wait_ge(xh_done, kt + 1)
                vec.tensor_tensor(xl[:, kt, :], ps[:, S0 + kt % 4, :], xh[:, kt, :], ALU.subtract).then_inc(xl_done, 1)

            for kt in range(HALF):
                x_low(kt)
            low(0, 0, 0)
            for kt in range(HALF, KT):
                x_low(kt)
            low(0, 0, 1)
            low(1, 1, 0)
            low(1, 1, 1)
            dve.wait_ge(cols_done, 5)

            def conv(i, n0, n1):
                for w in range(n0, n1):
                    o = odd[:, :] if w % 2 else y_tile(HEADS + i)
                    if w > 1:
                        dve.wait_ge(tap_done, i * TAPS + (w - 1))
                    tap = taps[:, ds(i, 1), w]
                    if w == 0:
                        ins = vec.tensor_scalar(o, u[:, 0:SEQ], tap, col(cn, B_DW, i), ALU.mult, ALU.add)
                    elif w == 1:
                        if not isinstance(i, int) or i:
                            dve.wait_ge(conv_done, i)
                        ins = vec.tensor_scalar(o, u[:, w:w + SEQ], tap, None, ALU.mult)
                    else:
                        ins = vec.scalar_tensor_tensor(out=o, in0=u[:, w:w + SEQ], scalar=tap, in1=o,
                                                       op0=ALU.mult, op1=ALU.add)
                    ins.then_inc(tap_done, 1)

            def conv_end(i):
                dve.wait_ge(tap_done, i * TAPS + TAPS)
                vec.tensor_tensor(y_tile(HEADS + i), y_tile(HEADS + i), odd[:, :], ALU.add).then_inc(conv_done, 1)

            def glu(i):
                dve.wait_ge(val_read, i + 1)
                dve.wait_ge(glu_tanh, i + 1)
                vec.scalar_tensor_tensor(out=u[:, PAD:], in0=tmp[:, :], scalar=1.0, in1=u[:, PAD:],
                                         op0=ALU.add, op1=ALU.mult).then_inc(u_done, 1)
                dve.wait_ge(u_done, i + 1)

            def body(i, i0):
                t = i * PER_HEAD + T_BODY
                at = [sum(BODY_TAPS[:s]) for s in range(PER_HEAD + 1)]

                def taps_of(s, part):
                    if i0:
                        return
                    mid = (at[s] + at[s + 1] + 1) // 2
                    lo, hi = (at[s], mid) if part == 0 else (mid, at[s + 1])
                    conv(i - 1, lo, min(hi, TAPS))
                    if lo < TAPS <= hi:
                        conv_end(i - 1)

                if i0:
                    forget()
                else:
                    glu(i - 1)
                for kind, (at_col, halved) in NOW.items():
                    ins = vec.tensor_copy(now[:, at_col:at_col + 1], col(hcols if halved else cols, kind, i))
                ins.then_inc(now_done, 1)
                low(t + 1, 0, 0)
                taps_of(0, 0)
                low(t + 1, 0, 1)
                taps_of(0, 1)
                dve.wait_ge(qk_high, i * 2 + 1)
                vec.scalar_tensor_tensor(out=ql, in0=ps[:, 1, :], scalar=col(cols, Q, i), in1=qh,
                                         op0=ALU.add, op1=ALU.subtract).then_inc(qk_low, 1)
                low(t + 2, 1, 0)
                taps_of(1, 0)
                low(t + 2, 1, 1)
                taps_of(1, 1)
                dve.wait_ge(qk_high, i * 2 + 2)
                vec.scalar_tensor_tensor(out=kl, in0=ps[:, 0, :], scalar=col(cols, K, i), in1=kh,
                                         op0=ALU.add, op1=ALU.subtract).then_inc(qk_low, 1)
                low(t + 3, 0, 0)
                taps_of(2, 0)
                low(t + 3, 0, 1)
                if not i0:
                    dve.wait_ge(negmax_done, i)
                for b in range(NT):
                    dve.wait_ge(scores_done, i * NT + (b + 1))
                    vec.reduce_max(row_max[:, b:b + 1], ps[:, S0 + b, 0:P * (b + 1)], AX.X).then_inc(max_done, 1)
                dve.wait_ge(max_done, i * NT + NT)
                vec.tensor_scalar(neg_max[:, :], row_max[:, :], -SCALE, None, ALU.mult).then_inc(negmax_done, 1)
                taps_of(2, 1)
                dve.wait_ge(exp_done, i * NT + NT)
                vec.reciprocal(row_inv[:, :], row_sum[:, :]).then_inc(inv_done, 1)
                dve.wait_ge(inv_done, i + 1)
                for b in range(NT):
                    pr = probs[:, PR_AT[b]:PR_AT[b + 1]]
                    vec.tensor_scalar(pr, pr, row_inv[:, b:b + 1], None, ALU.mult).then_inc(probs_done, 1)
                low(t + 4, 1, 0)
                taps_of(3, 0)
                low(t + 4, 1, 1)
                dve.wait_ge(vh_done, i + 1)
                vec.tensor_tensor(vl[:, :], ps[:, V_BANK, :], vh[:, :], ALU.subtract).then_inc(vl_done, 1)
                taps_of(3, 1)
                dve.wait_ge(gate_read, i * 2 + 2)
                vec.scalar_tensor_tensor(out=y_tile(i), in0=tmp[:, :], scalar=1.0, in1=v_t[:, :],
                                         op0=ALU.add, op1=ALU.mult).then_inc(gate_done, 1)
                low(t + 5, 0, 0)
                taps_of(4, 0)
                low(t + 5, 0, 1)
                for j in range(NT):
                    dve.wait_ge(pth_done, i * NT + (j + 1))
                    c = slice(PT_AT[j], PT_AT[j + 1])
                    vec.tensor_tensor(ptl[:, c], ps[:, S0 + j, 0:PT_N[j]], pth[:, c], ALU.subtract).then_inc(ptl_done, 1)
                taps_of(4, 1)
                low(t + 6, 1, 0)
                low(t + 6, 1, 1)
                dve.wait_ge(pv_done, i + 1)
                dve.wait_ge(gate_done, i + 1)
                vec.tensor_tensor(y_tile(i), ps[:, O_BANK, :], y_tile(i), ALU.mult).then_inc(attn_done, 1)

            def forget():
                dve.wait_ge(f_act, 4)
                vec.scalar_tensor_tensor(out=fm, in0=fz, scalar=0.0, in1=fa, op0=ALU.min, op1=ALU.subtract) \
                   .then_inc(f_vec, 1)
                dve.wait_ge(f_vec, 1)
                vec.tensor_tensor_scan(fcum, one_row, fm, 0.0, ALU.mult, ALU.add).then_inc(f_vec, 1)
                dve.wait_ge(f_vec, 2)
                vec.tensor_scalar(fcum, fcum, 1.0 / SCALE, None, ALU.mult).then_inc(f_vec, 1)
                dve.wait_ge(f_act, 5)
                vec.tensor_tensor(cum4[:, SEQ:2 * SEQ].bitcast(F32R), fcum, cum4[:, 0:SEQ], ALU.subtract).then_inc(f_vec, 1)
                vec.tensor_scalar(cum4[:, 2 * SEQ:3 * SEQ], cum4[:, 0:SEQ], -1.0, None, ALU.mult).then_inc(f_vec, 1)
                dve.wait_ge(f_vec, 5)
                vec.tensor_scalar(cum4[:, 3 * SEQ:4 * SEQ], cum4[:, SEQ:2 * SEQ], -1.0, None, ALU.mult).then_inc(f_vec, 2)

            one_row = odd[0:HEADS, :]
            vec.memset(one_row, 1.0).then_inc(vec_const, 1)
            dve.wait_ge(vec_const, 7)

            body(0, True)
            with vec.Fori(1, HEADS) as i:
                body(i, False)

            def bias_z(j, par):
                if not isinstance(j, int) or j >= 2:
                    dve.wait_ge(z_read, j * 2 - 2)
                vec.tensor_copy(now_z[:, par:par + 1], col(hcols, GATE_C, j)).then_inc(nowz_done, 1)

            def gate(j, slot):
                dve.wait_ge(z_read, j * 2 + 2)
                vec.scalar_tensor_tensor(out=zbuf[:, slot, :], in0=tmp[:, :], scalar=1.0, in1=zbuf[:, slot, :],
                                         op0=ALU.add, op1=ALU.mult).then_inc(z_done, 1)

            def normed(j):
                dve.wait_ge(rstd_vec, 6)
                if not isinstance(j, int) or j:
                    dve.wait_ge(aff_done, j * 2)
                vec.tensor_copy(now_n[:, 0:1], hcn[:, ds(G_CN * HEADS + j, 1)]).then_inc(nown_done, 1)
                vec.tensor_copy(now_n[:, 1:2], hcn[:, ds(B_CN * HEADS + j, 1)]).then_inc(nown_done, 1)
                dve.wait_ge(nown_done, j * 2 + 2)
                vec.tensor_tensor(sq[:, 0, :], y_tile(HEADS + j), rstd[:, :], ALU.mult).then_inc(norm_done, 1)

            def gated(j, slot):
                dve.wait_ge(aff_done, j * 2 + 2)
                vec.scalar_tensor_tensor(out=y_tile(HEADS + j), in0=odd[:, :], scalar=1.0, in1=sq[:, 1, :],
                                         op0=ALU.add, op1=ALU.mult).then_inc(act_done, 1)
                dve.wait_ge(act_done, j + 1)
                dve.wait_ge(z_done, j + 1)
                vec.tensor_tensor(y_tile(HEADS + j), y_tile(HEADS + j), zbuf[:, slot, :], ALU.mult).then_inc(yc_done, 1)

            t, c = T_GATE, HEADS - 1
            for j in range(2):
                bias_z(j, (j + 1) % 2)
            glu(c)
            low(t + 1, 0, 0)
            conv(c, 0, 6)
            low(t + 1, 0, 1)
            conv(c, 6, 16)
            gate(0, 0)
            bias_z(2, 1)
            low(t + 2, 1, 0)
            conv(c, 16, 24)
            low(t + 2, 1, 1)
            conv(c, 24, TAPS)
            conv_end(c)
            gate(1, 1)
            bias_z(3, 0)
            low(t + 3, 0, 0)
            low(t + 3, 0, 1)
            vec.memset(sq_odd[:, :], 0.0).then_inc(sqo_done, 1)

            def center(j):
                vec.tensor_tensor(y_tile(HEADS + j), y_tile(HEADS + j), ps[:, V_BANK, :], ALU.subtract).then_inc(cent_done, 1)

            def add_square(j):
                dve.wait_ge(sq_done, j + 1)
                dve.wait_ge(sqo_done, (j - 1) // 2 + 1)
                vec.tensor_tensor(sq_odd[:, :], sq_odd[:, :], sq[:, j % 3, :], ALU.add).then_inc(sqo_done, 1)

            dve.wait_ge(mean_done, 1)
            for j in range(HEADS):
                center(j)
                if j >= 4 and j % 2 == 0:
                    add_square(j - 3)
                if j == 8:
                    gate(2, 2)
                    low(t + 4, 1, 0)
                    low(t + 4, 1, 1)
            add_square(HEADS - 3)
            add_square(HEADS - 1)

            def root():
                dve.wait_ge(var_done, 1)
                vec.tensor_scalar(sq_odd[:, :], ps[:, O_BANK, :], LN_EPS, None, ALU.add).then_inc(rstd_vec, 1)
                dve.wait_ge(rstd_act, 2)
                vec.tensor_tensor(odd[:, :], rstd[:, :], rstd[:, :], ALU.mult).then_inc(rstd_vec, 1)
                dve.wait_ge(rstd_vec, 2)
                vec.tensor_tensor(odd[:, :], odd[:, :], sq_odd[:, :], ALU.mult).then_inc(rstd_vec, 1)
                dve.wait_ge(rstd_vec, 3)
                vec.tensor_scalar(odd[:, :], odd[:, :], -0.5, 1.5, ALU.mult, ALU.add).then_inc(rstd_vec, 1)
                dve.wait_ge(rstd_vec, 4)
                vec.tensor_tensor(rstd[:, :], rstd[:, :], odd[:, :], ALU.mult).then_inc(rstd_vec, 2)

            def gate_step(j, s):
                gate(j - 1, (s - 1) % 4)
                bias_z(j, (s + 1) % 2)
                low(j + (T_GATE + 1), s % 2, 0)
                if isinstance(j, int) and j == 4:
                    low(j + (T_GATE + 1), s % 2, 1)
                    root()
                    normed(j - 4)
                else:
                    normed(j - 4)
                    low(j + (T_GATE + 1), s % 2, 1)
                gated(j - 4, s)

            for j in range(4, 8):
                gate_step(j, j % 4)
            with vec.Fori(2, HEADS // 4) as b:
                for s in range(4):
                    gate_step(b * 4 + s, s)

            def split_y(n, slot, src):
                dve.wait_ge(yh_done, n + 1)
                vec.tensor_tensor(yl[:, slot, :], src, yh[:, slot, :], ALU.subtract).then_inc(yl_done, 1)

            def out_pair(pair, m, s, nxt, conv_tile=None):
                t = pair + T_OUT
                if conv_tile is not None:
                    normed(conv_tile)
                low(t + 1, s, 0)
                split_y(pair * 2 + 1, 1, y_tile(m * 2 + 1))
                if conv_tile is not None:
                    gated(conv_tile, conv_tile % 4)
                low(t + 1, s, 1)
                split_y(pair * 2 + 2, 0, y_tile(nxt))

            split_y(0, 0, y_tile(0))
            gate(HEADS - 1, 3)
            for m in range(4):
                out_pair(m, m, m % 2, 2 * m + 2, HEADS - 4 + m)
            with vec.Fori(2, OUT_PAIRS // 2 - 1) as b:
                for s in range(2):
                    out_pair(b * 2 + s, b * 2 + s, s, b * 4 + (2 * s + 2))
            out_pair(OUT_PAIRS - 2, OUT_PAIRS - 2, 0, 2 * OUT_PAIRS - 2)
            out_pair(OUT_PAIRS - 1, OUT_PAIRS - 1, 1, 0)

            def add_result(p, n):
                for g in range(2):
                    r = res[:, n, 1024 * p + SEQ * g:1024 * p + SEQ * (g + 1)]
                    vec.tensor_tensor(r, ps[:, (2 * n + g + 2) % 8, :], r, ALU.add).then_inc(evac_done, 1)

            def row_stats(p, n):
                dve.wait_ge(evac_done, 8 * p + 2 * n + 2)
                for g in range(2 * p, 2 * p + 2):
                    ins = vec.bn_stats(stats[:, n, g, :], res[:, n, SEQ * g:SEQ * (g + 1)])
                return ins

            dve.wait_ge(res_ready, NT)
            for n in range(NT):
                if n < NT - 1:
                    dve.wait_ge(sum_done, n + 1)
                else:
                    dve.wait_ge(half_done, 2 * T_OUT + 2 * OUT_PAIRS)
                add_result(0, n)
            for m in range(4):
                out_pair(OUT_PAIRS + m, m, m % 2, 2 * m + 2)
                row_stats(0, m).then_inc(stats_done, 1)
            with vec.Fori(2, OUT_PAIRS // 2 - 1) as b:
                for s in range(2):
                    out_pair(b * 2 + (OUT_PAIRS + s), b * 2 + s, s, b * 4 + (2 * s + 2))
            t = T_OUT + N_OUT - 2
            low(t + 1, 0, 0)
            split_y(2 * N_OUT - 3, 1, y_tile(2 * OUT_PAIRS - 3))
            low(t + 1, 0, 1)
            for n in range(2):
                dve.wait_ge(yh_done, 2 * N_OUT - 1 + n)
                vec.tensor_tensor(yl_end[:, n, :], y_tile(2 * OUT_PAIRS - 2 + n), yh_end[:, n, :], ALU.subtract) \
                   .then_inc(yl_done, 1)

            dve.wait_ge(bcast_loaded, 48)
            dve.wait_ge(stats_done, NT)
            for n in range(NT):
                base = FIN * n
                dve.wait_ge(half_done, 2 * T_OUT + 2 * N_OUT - 4 + n + 1)
                add_result(1, n)
                row_stats(1, n).then_inc(fin_vec, 1)
                dve.wait_ge(fin_vec, base + 1)
                if n:
                    dve.wait_ge(row_done, 2 * n)
                vec.bn_aggr(mv[:, :], stats[:, n, :, :].rearrange("p a b -> p (a b)")).then_inc(fin_vec, 2)
                dve.wait_ge(fin_vec, base + 3)
                vec.tensor_scalar(var_eps[:, :], mv[:, 1:2], LN_EPS, None, ALU.add).then_inc(fin_vec, 1)
                for h in range(2):
                    r, c = res[:, n, 1024 * h:1024 * (h + 1)], slice(1024 * h, 1024 * (h + 1))
                    vec.scalar_tensor_tensor(out=r, in0=r, scalar=mv[:, 0:1], in1=gpost_b[:, c],
                                             op0=ALU.subtract, op1=ALU.mult).then_inc(scaled_done, 1)
                dve.wait_ge(fin_act, n + 1)
                vec.reciprocal(rs[:, :], std[:, :]).then_inc(fin_vec, 1)
                dve.wait_ge(fin_vec, base + 5)
                vec.scalar_tensor_tensor(out=newton[:, :], in0=rs[:, :], scalar=var_eps[:, :], in1=rs[:, :],
                                         op0=ALU.mult, op1=ALU.mult).then_inc(fin_vec, 1)
                dve.wait_ge(fin_vec, base + 6)
                vec.tensor_scalar(newton[:, :], newton[:, :], -0.5, 1.5, ALU.mult, ALU.add).then_inc(fin_vec, 1)
                dve.wait_ge(fin_vec, base + 7)
                vec.tensor_tensor(rs[:, :], rs[:, :], newton[:, :], ALU.mult).then_inc(fin_vec, 1)
                dve.wait_ge(fin_vec, base + 8)
                dve.wait_ge(scaled_done, 2 * n + 2)
                for h in range(2):
                    r, c = res[:, n, 1024 * h:1024 * (h + 1)], slice(1024 * h, 1024 * (h + 1))
                    vec.scalar_tensor_tensor(out=r, in0=r, scalar=rs[:, :], in1=bpost_b[:, c],
                                             op0=ALU.mult, op1=ALU.add).then_inc(row_done, 1)


_INS = ["x", "w_in", "b_in", "w_dw", "b_dw", "g_conv_norm", "b_conv_norm", "w_out", "b_out", "g_post", "b_post"]


def kernel(**inputs):
    import numpy as np
    import concourse.bacc as bacc
    from concourse.bass_utils import run_bass_kernel_spmd

    nc = bacc.Bacc("TRN2", target_bir_lowering=False, num_devices=1)
    arrays, args = {}, []
    for name in _INS:
        a = np.ascontiguousarray(inputs[name])
        arrays[f"in_{name}_dram"] = a
        args.append(nc.dram_tensor(f"in_{name}_dram", a.shape, mybir.dt.from_np(a.dtype), kind="ExternalInput").ap())
    out = nc.dram_tensor("out_0_dram", (1, SEQ, D), F32, kind="ExternalOutput").ap()
    scratch = nc.dram_tensor("forget_sums_dram", (HEADS, 4 * SEQ), F32).ap()
    build(nc, *args, out, scratch)
    r = run_bass_kernel_spmd(nc, [arrays], core_ids=[0])
    return r.results[0]["out_0_dram"]
```

```python
import math
from contextlib import ExitStack

import concourse.bass as bass
from concourse import mybir

F32 = mybir.dt.float32
F32R = mybir.dt.float32r
ACT = mybir.ActivationFunctionType
ALU = mybir.AluOpType

P = 128
SEQ = 512
D = 2048
KT = D // P
HALF = KT // 2
NT = SEQ // P
HEADS = D // P
TAPS = 31
PAD = TAPS - 1
LN_EPS = 1e-5
ALPHA = 2.0 ** 0.25
SCALE = 1.0 / math.sqrt(P)
MASKED = -1e37

PER_HEAD = 6
T_BODY = 1
T_GATE = T_BODY + PER_HEAD * HEADS
T_OUT = T_GATE + HEADS
OUT_PAIRS = HEADS
N_OUT = 2 * OUT_PAIRS
FIN = 8
X_CUTS = (0, P, 2 * P, 4 * P, 6 * P, 9 * P, 12 * P, D)
LOW_AT, F_WIDE = 32, 64
SLOTS = 4
OUT_STEPS = 2 * N_OUT
PER_PASS = 2 * OUT_PAIRS
END = 8
E0 = OUT_STEPS - END

VAL, GLU, GATE_C, Q, K, V, GATE_A = range(7)
F_COL = 6 * D
BODY_KINDS = (Q, K, V, GATE_A, VAL, GLU)
BODY_TAPS = (7, 7, 7, 6, 5, 0)
B_DW, G_CN, B_CN = range(3)
NOW = {Q: (0, False), K: (1, False), V: (2, False), GATE_A: (3, True), VAL: (4, True), GLU: (5, True)}

PT_N = [SEQ - P * j for j in range(NT)]
PT_AT = [sum(PT_N[:j]) for j in range(NT + 1)]
PR_AT = [P * i * (i + 1) // 2 for i in range(NT + 1)]


def col_of(kind, i):
    return (F_COL + HEADS if kind == GATE_A else kind * D) + P * i


def build(nc, x, w_in, b_in, w_dw, b_dw, g_cn, b_cn, w_out, b_out, g_post, b_post, out, scratch):
    ctx = ExitStack()
    with ctx:
        def sb(name, shape, dt=F32, where=ctx):
            return where.enter_context(nc.sbuf_tensor(name, shape, dt))

        def sem(name):
            return ctx.enter_context(nc.semaphore(name))

        ends = ExitStack()
        wh_last = sb("wh_last", [P, 4, HALF * P], F32R, ends)
        wl_last = sb("wl_last", [P, 4, HALF * P], F32R, ends)
        ends.close()
        y = sb("y", [P, 2 * HEADS, SEQ])
        y_flat = y[:, :, :].rearrange("p a b -> p (a b)")
        raw = sb("raw", [P, 2, HALF * P])
        wh = sb("wh", [P, SLOTS, HALF * P], F32R)
        wl = sb("wl", [P, SLOTS, HALF * P], F32R)
        u = sb("u", [P, PAD + SEQ])
        tmp = sb("tmp", [P, SEQ])
        odd = sb("odd", [P, SEQ])
        csum = sb("csum", [P, SEQ])
        ident = sb("ident", [P, P])
        mask = sb("mask", [P, P])
        mean_w = sb("mean_w", [P, P])
        cols = sb("cols", [P, 7 * HEADS])
        hcols = sb("hcols", [P, 7 * HEADS])
        cn = sb("cn", [P, 3 * HEADS])
        hcn = sb("hcn", [P, 3 * HEADS])
        taps = sb("taps", [P, HEADS, TAPS])
        now = sb("now", [P, 6])
        now_z = sb("now_z", [P, 2])
        now_n = sb("now_n", [P, 2])
        fbias = sb("fbias", [HEADS, 1])
        one = sb("one", [P, 1])
        row_max = sb("row_max", [P, NT])
        waited = sb("waited", [P, NT])
        neg_max = sb("neg_max", [P, NT])
        row_sum = sb("row_sum", [P, NT])
        row_inv = sb("row_inv", [P, NT])
        stats = sb("stats", [P, NT, 4, 6])
        mv = sb("mv", [P, 2])
        var_eps = sb("var_eps", [P, 1])
        std = sb("std", [P, 1])
        rs = sb("rs", [P, 1])
        newton = sb("newton", [P, 1])

        first = ExitStack()
        parts = sb("parts", [P, 2 * PT_AT[NT]], F32R, first)
        v_t = sb("v_t", [P, SEQ], F32, first)
        vh = sb("vh", [P, NT * P], F32R, first)
        vl = sb("vl", [P, NT * P], F32R, first)
        probs = sb("probs", [P, PR_AT[NT]], F32, first)
        cum_t = sb("cum_t", [P, HEADS, NT], F32, first)
        now_cum = sb("now_cum", [P, NT], F32, first)
        first.close()
        yh_last = sb("yh_last", [P, 4, SEQ], F32R, first)
        yl_last = sb("yl_last", [P, 4, SEQ], F32R, first)
        first.close()
        zbuf = sb("zbuf", [P, 4, SEQ])
        sq = sb("sq", [P, 3, SEQ])
        sq_odd = sb("sq_odd", [P, SEQ])
        yh = sb("yh", [P, 2, SEQ], F32R)
        yl = sb("yl", [P, 2, SEQ], F32R)
        rstd = sb("rstd", [P, SEQ])
        second = ExitStack()
        xh = sb("xh", [P, KT, SEQ], F32R, second)
        xl = sb("xl", [P, KT, SEQ], F32R, second)
        second.close()
        res = sb("res", [P, NT, D])
        bout_b = sb("bout_b", [P, D])
        gpost_b = sb("gpost_b", [P, D])
        bpost_b = sb("bpost_b", [P, D])
        yh_end = sb("yh_end", [P, 2, SEQ], F32R)
        yl_end = sb("yl_end", [P, 2, SEQ], F32R)

        ps = ctx.enter_context(nc.psum_tensor("ps", [P, 8, SEQ], F32))
        S0, V_BANK, O_BANK = 2, 6, 7
        qh, ql, kh, kl = (parts[:, SEQ * n:SEQ * (n + 1)] for n in range(4))
        pth, ptl = parts[:, 0:PT_AT[NT]], parts[:, PT_AT[NT]:]
        x_rows = y_flat[:, 0:NT * D].rearrange("p (t d) -> p t d", t=NT)
        rows = y_flat[:, NT * D:]
        neg_cum = y_flat[0:HEADS, 12 * SEQ:13 * SEQ]
        f_raw = [raw[:, h, 0:HALF * HEADS].rearrange("p (k c) -> p k c", k=HALF) for h in range(2)]
        f_w = [wh[:, h, 0:HALF * F_WIDE].rearrange("p (k c) -> p k c", k=HALF) for h in range(2)]
        f_low = v_t[0:HEADS, :]
        fz, fa = probs[0:HEADS, 0:SEQ], probs[0:HEADS, SEQ:2 * SEQ]
        fm, fcum = u[0:HEADS, PAD:], tmp[0:HEADS, :]

        def end_y(ring, last, end, q):
            return last[:, q, :] if q < 4 else ring[:, q % 2, :] if q < 6 else end[:, q - 6, :]

        x_loaded = [sem(f"x_loaded{n}") for n in range(len(X_CUTS) - 1)]
        rows_loaded, bcast_loaded, stored = sem("rows_loaded"), sem("bcast_loaded"), sem("stored")
        raw_full = [sem("raw_full0"), sem("raw_full1")]
        cum_stored, bias_loaded = sem("cum_stored"), sem("bias_loaded")
        cum_turned, cum_t_done, now_cum_done = sem("cum_turned"), sem("cum_t_done"), sem("now_cum_done")
        bias_summed, bias_done = sem("bias_summed"), sem("bias_done")
        res_loaded = sem("res_loaded")
        const_done, vec_const = sem("const_done"), sem("vec_const")
        xt_turned, xh_done, xl_done = sem("xt_turned"), sem("xh_done"), sem("xl_done")
        cols_turned, cols_done = sem("cols_turned"), sem("cols_done")
        high_done, low_done, half_done = sem("high_done"), sem("low_done"), sem("half_done")
        f_act, f_vec, f_pad = sem("f_act"), sem("f_vec"), sem("f_pad")
        qk_high, qk_low = sem("qk_high"), sem("qk_low")
        vt_done, v_turned, vh_done, vl_done = sem("vt_done"), sem("v_turned"), sem("vh_done"), sem("vl_done")
        scores_done, max_done, negmax_done = sem("scores_done"), sem("max_done"), sem("negmax_done")
        exp_done, inv_done, probs_done = sem("exp_done"), sem("inv_done"), sem("probs_done")
        p_turned, pth_done, ptl_done, pv_done = sem("p_turned"), sem("pth_done"), sem("ptl_done"), sem("pv_done")
        now_done, nowz_done, nown_done = sem("now_done"), sem("nowz_done"), sem("nown_done")
        gate_read, gate_done, attn_done = sem("gate_read"), sem("gate_done"), sem("attn_done")
        val_read, glu_tanh, u_done, tap_done = sem("val_read"), sem("glu_tanh"), sem("u_done"), sem("tap_done")
        conv_done, csum_done, mean_done = sem("conv_done"), sem("csum_done"), sem("mean_done")
        cent_done, sq_done, sqe_done, sqo_done = sem("cent_done"), sem("sq_done"), sem("sqe_done"), sem("sqo_done")
        var_done, rstd_act, rstd_vec = sem("var_done"), sem("rstd_act"), sem("rstd_vec")
        z_read, z_done = sem("z_read"), sem("z_done")
        norm_done, aff_done, act_done, yc_done = sem("norm_done"), sem("aff_done"), sem("act_done"), sem("yc_done")
        yh_done, yl_done = sem("yh_done"), sem("yl_done")
        res_scaled, res_ready, evac_done = sem("res_scaled"), sem("res_ready"), sem("evac_done")
        fin_vec, fin_act, row_done = sem("fin_vec"), sem("fin_act"), sem("row_done")
        sum_done = sem("sum_done")
        stats_done, scaled_done = sem("stats_done"), sem("scaled_done")

        block = ctx.enter_context(nc.Block())

        def ds(i, n):
            return bass.ds(i, n)

        @block.sync
        def _(sp):
            def load_in(t, col, second_first=False):
                for h in (1, 0) if second_first else (0, 1):
                    if not (second_first and h == 0):
                        sp.wait_ge(low_done, 2 * t + h - 1)
                    src = w_in[D // 2 * h:D // 2 * (h + 1), ds(col, P)]
                    sp.dma_start(raw[:, h, :].rearrange("p (k c) -> p k c", k=HALF),
                                 src.rearrange("(k p) c -> p k c", p=P)).then_inc(raw_full[h], 16)

            def load_out(t, row, half_cols):
                for h in range(2):
                    sp.wait_ge(low_done, 2 * t + h - 1)
                    sp.dma_start(raw[:, h, :], w_out[ds(row + P * h, P), half_cols * 1024:half_cols * 1024 + 1024]) \
                      .then_inc(raw_full[h], 16)

            def load_bias(h):
                with nc.allow_non_contiguous_dma(reason="a row repeated over the partitions"):
                    for b in range(NT):
                        row = scratch[ds(h, 1), 0:P * (b + 1)].rearrange("a n -> (a n)")
                        sp.dma_start(probs[:, PR_AT[b]:PR_AT[b + 1]], row.partition_broadcast(P)).then_inc(bias_loaded, 16)

            def load_first(h):
                src = w_in[D // 2 * h:D // 2 * (h + 1), F_COL:F_COL + HEADS]
                sp.dma_start(f_raw[h], src.rearrange("(k p) c -> p k c", p=P)).then_inc(raw_full[h], 16)

            x_v = x.rearrange("a (t p) d -> p (a t) d", p=P)
            for n, (lo, hi) in enumerate(zip(X_CUTS, X_CUTS[1:])):
                sp.dma_start(x_rows[:, :, lo:hi], x_v[:, :, lo:hi]).then_inc(x_loaded[n], 16)
                if n == 0:
                    with nc.allow_non_contiguous_dma(reason="16 columns of w_in"):
                        load_first(0)
                        load_first(1)
            sp.dma_start(rows[0:TAPS, 0:D], w_dw).then_inc(rows_loaded, 16)
            sp.dma_start(rows[0:6 * HEADS, D:D + P], b_in[0:6 * D].rearrange("(j p) -> j p", p=P)).then_inc(rows_loaded, 16)
            sp.dma_start(rows[6 * HEADS:7 * HEADS, D:D + P],
                         b_in[F_COL + HEADS:F_COL + HEADS + D].rearrange("(j p) -> j p", p=P)).then_inc(rows_loaded, 16)
            for n, vec in enumerate((b_dw, g_cn, b_cn)):
                sp.dma_start(rows[n * HEADS:(n + 1) * HEADS, D + P:D + 2 * P],
                             vec.rearrange("(j p) -> j p", p=P)).then_inc(rows_loaded, 16)
            sp.dma_start(fbias[:, :], b_in[F_COL:F_COL + HEADS].rearrange("(j p) -> j p", p=1)).then_inc(rows_loaded, 16)
            load_in(1, col_of(Q, 0))

            def body(i, first=False):
                for s, kind in enumerate(BODY_KINDS):
                    t = i * PER_HEAD + (T_BODY + s)
                    if s + 1 < PER_HEAD:
                        load_in(t + 1, col_of(BODY_KINDS[s + 1], 0) + i * P, BODY_KINDS[s + 1] == VAL)
                    if s == 1 and first:
                        sp.wait_ge(f_vec, 4)
                        sp.dma_start(scratch, neg_cum).then_inc(cum_stored, 16)
                        sp.wait_ge(cum_stored, 16)
                        load_bias(0)

            def next_bias(i):
                sp.wait_ge(p_turned, i * NT + NT)
                load_bias(i + 1)

            body(0, True)
            next_bias(0)
            load_in(T_BODY + PER_HEAD, col_of(Q, 1))
            with nc.sync.Fori(1, HEADS - 1) as i:
                body(i)
                next_bias(i)
                load_in(i * PER_HEAD + (T_BODY + PER_HEAD), col_of(Q, 1) + i * P)
            i = HEADS - 1
            for s in range(1, PER_HEAD):
                load_in(T_BODY + i * PER_HEAD + s, col_of(BODY_KINDS[s], i))
            with nc.sync.Fori(0, HEADS) as j:
                load_in(j + T_GATE, col_of(GATE_C, 0) + j * P)
            for p in range(2):
                t = T_OUT + p * OUT_PAIRS
                with nc.sync.Fori(0, OUT_PAIRS // 2) as m:
                    load_out(m + t, D + m * (2 * P), p)
                with nc.sync.Fori(0, OUT_PAIRS // 2) as m:
                    load_out(m + (t + OUT_PAIRS // 2), m * (2 * P), p)
            for t in range(NT):
                for h in range(2):
                    c = slice(1024 * h, 1024 * (h + 1))
                    sp.wait_ge(row_done, 2 * t + h + 1)
                    sp.dma_start(out[0, P * t:P * (t + 1), c], res[:, t, c]).then_inc(stored, 16)
            sp.wait_ge(stored, 32 * NT)

        @block.gpsimd
        def _(pool):
            nc.gpsimd.memset(ident[:, :], 0.0).then_inc(const_done, 1)
            nc.gpsimd.memset(mask[:, :], 0.0).then_inc(const_done, 1)
            pool.wait_ge(const_done, 2)
            nc.gpsimd.affine_select(out=ident[:, :], in_=ident[:, :], compare_op=ALU.not_equal, fill=1.0,
                                    base=0, pattern=[[-1, P]], channel_multiplier=1).then_inc(const_done, 1)
            nc.gpsimd.affine_select(out=mask[:, :], in_=mask[:, :], compare_op=ALU.is_ge, fill=MASKED,
                                    base=0, pattern=[[-1, P]], channel_multiplier=1).then_inc(const_done, 1)
            pool.wait_ge(const_done, 4)
            pool.wait_ge(vec_const, 4)

            def bias(i):
                pool.wait_ge(bias_loaded, i * (16 * NT) + 16 * NT)
                pool.wait_ge(now_cum_done, i + 1)
                for b in range(NT):
                    o = probs[:, PR_AT[b]:PR_AT[b + 1]]
                    nc.gpsimd.tensor_tensor(o, o, now_cum[:, b:b + 1].to_broadcast([P, P * (b + 1)]), ALU.add) \
                      .then_inc(bias_summed, 1)
                for b in range(NT):
                    pool.wait_ge(bias_summed, i * NT + (b + 1))
                    o = probs[:, PR_AT[b + 1] - P:PR_AT[b + 1]]
                    nc.gpsimd.tensor_tensor(o, o, mask[:, :], ALU.add).then_inc(bias_done, 1)

            def add_conv(i):
                pool.wait_ge(conv_done, i + 1)
                if not isinstance(i, int) or i:
                    pool.wait_ge(csum_done, i)
                nc.gpsimd.tensor_tensor(csum[:, :], csum[:, :], y[:, ds(HEADS + i, 1), :].rearrange("p a b -> p (a b)"),
                                        ALU.add).then_inc(csum_done, 1)

            bias(0)
            bias(1)
            add_conv(0)
            with nc.gpsimd.Fori(2, HEADS) as i:
                bias(i)
                add_conv(i - 1)
            add_conv(HEADS - 1)
            pool.wait_ge(mean_done, 1)
            nc.gpsimd.memset(csum[:, :], 0.0).then_inc(sqe_done, 1)
            for j in range(0, HEADS, 2):
                pool.wait_ge(sq_done, j + 1)
                pool.wait_ge(sqe_done, j // 2 + 1)
                nc.gpsimd.tensor_tensor(csum[:, :], csum[:, :], sq[:, j % 3, :], ALU.add).then_inc(sqe_done, 1)

            def repeat_row(step, dst, src):
                pool.wait_ge(half_done, 2 * T_OUT + step)
                with nc.allow_non_contiguous_dma(reason="a row repeated over the partitions"):
                    nc.gpsimd.dma_start(dst[:, :], src.partition_broadcast(P)).then_inc(bcast_loaded, 16)

            repeat_row(1, bout_b, b_out)
            for t in range(NT):
                pool.wait_ge(half_done, 2 * T_OUT + 4 * (t + 1))
                nc.gpsimd.dma_start(res[:, t, :], x[0, P * t:P * (t + 1), :]).then_inc(res_loaded, 16)
                pool.wait_ge(res_loaded, 16 * (t + 1))
                nc.gpsimd.tensor_scalar(res[:, t, :], res[:, t, :], ALPHA, None, ALU.mult).then_inc(res_scaled, 1)
                pool.wait_ge(res_scaled, t + 1)
                if t == 0:
                    pool.wait_ge(bcast_loaded, 16)
                nc.gpsimd.tensor_tensor(res[:, t, :], res[:, t, :], bout_b[:, :], ALU.add).then_inc(res_ready, 1)
            repeat_row(24, gpost_b, g_post)
            repeat_row(28, bpost_b, b_post)

        @block.scalar
        def _(act):
            def high(t, par, h, lag=4):
                act.wait_ge(raw_full[h], 16 * (t + 1))
                if not isinstance(t, int) or t >= 2:
                    act.wait_ge(half_done, 2 * t + (h + 1 - lag))
                nc.scalar.activation(wh[:, 2 * par + h, :], raw[:, h, :], ACT.Copy).then_inc(high_done, 1)

            def bank_of(par):
                return ps[:, par, :]

            def bias_of(kind):
                return now[:, NOW[kind][0]:NOW[kind][0] + 1]

            def tile_done(t):
                act.wait_ge(half_done, 2 * t + 2)

            def x_high(kt):
                act.wait_ge(xt_turned, kt + 1)
                nc.scalar.activation(xh[:, kt, :], ps[:, S0 + kt % 4, :], ACT.Copy).then_inc(xh_done, 1)

            for kt in range(KT):
                x_high(kt)
                if kt in (1, 2):
                    h = kt - 1
                    act.wait_ge(raw_full[h], 16)
                    nc.scalar.activation(f_w[h][:, :, 0:HEADS], f_raw[h], ACT.Copy).then_inc(high_done, 1)
            high(1, 1, 0)
            high(1, 1, 1)
            act.wait_ge(cols_turned, 1)
            nc.scalar.activation(cols[:, :], ps[:, V_BANK, 0:7 * HEADS], ACT.Copy).then_inc(cols_done, 1)
            nc.scalar.activation(hcols[:, :], ps[:, V_BANK, 0:7 * HEADS], ACT.Copy, scale=0.5).then_inc(cols_done, 1)
            nc.scalar.activation(cn[:, :], ps[:, V_BANK, 128:128 + 3 * HEADS], ACT.Copy).then_inc(cols_done, 1)
            nc.scalar.activation(hcn[:, :], ps[:, V_BANK, 128:128 + 3 * HEADS], ACT.Copy, scale=0.5).then_inc(cols_done, 1)
            act.wait_ge(cols_turned, 2)
            nc.scalar.activation(taps[:, :, :].rearrange("p a b -> p (a b)"), ps[:, O_BANK, 0:HEADS * TAPS],
                                 ACT.Copy).then_inc(cols_done, 1)
            act.wait_ge(cols_done, 5)

            tile_done(0)
            act.wait_ge(vec_const, 2)
            nc.scalar.activation(f_low, ps[LOW_AT:LOW_AT + HEADS, 0, :], ACT.Copy).then_inc(f_act, 1)
            act.wait_ge(f_vec, 1)
            nc.scalar.activation(fa, fz, ACT.Abs).then_inc(f_act, 1)
            act.wait_ge(f_act, 2)
            nc.scalar.activation(fa, fa, ACT.Exp, scale=-1.0).then_inc(f_act, 1)
            act.wait_ge(f_act, 3)
            nc.scalar.activation(fa, fa, ACT.Ln, bias=one[0:HEADS, :]).then_inc(f_act, 1)

            def glu_gate(t, i):
                tile_done(t)
                act.wait_ge(gate_done, i + 1)
                nc.scalar.activation(tmp[:, :], bank_of(0), ACT.Tanh, bias=bias_of(GLU), scale=0.5) \
                  .then_inc(glu_tanh, 1)

            def body(i, i0):
                t = i * PER_HEAD + T_BODY
                if not i0:
                    glu_gate(t - 1, i - 1)
                high(t + 1, 0, 0)
                high(t + 1, 0, 1)
                tile_done(t)
                if not i0:
                    act.wait_ge(pv_done, i)
                act.wait_ge(now_done, i + 1)
                nc.scalar.activation(qh, bank_of(1), ACT.Identity, bias=bias_of(Q)).then_inc(qk_high, 1)
                high(t + 2, 1, 0)
                high(t + 2, 1, 1)
                tile_done(t + 1)
                nc.scalar.activation(kh, bank_of(0), ACT.Identity, bias=bias_of(K)).then_inc(qk_high, 1)
                high(t + 3, 0, 0)
                high(t + 3, 0, 1)
                act.wait_ge(negmax_done, i + 1)
                for b in range(NT):
                    o = probs[:, PR_AT[b]:PR_AT[b + 1]]
                    nc.scalar.activation(o, o, ACT.Exp,
                                         bias=neg_max[:, b:b + 1], scale=SCALE,
                                         accum_out=row_sum[:, b:b + 1]).then_inc(exp_done, 1)
                tile_done(t + 2)
                nc.scalar.activation(v_t[:, :], bank_of(1), ACT.Identity, bias=bias_of(V)).then_inc(vt_done, 1)
                high(t + 4, 1, 0)
                high(t + 4, 1, 1)
                act.wait_ge(v_turned, i + 1)
                nc.scalar.activation(vh[:, :], ps[:, V_BANK, :], ACT.Copy).then_inc(vh_done, 1)
                tile_done(t + 3)
                nc.scalar.activation(v_t[:, :], bank_of(0), ACT.Identity,
                                     bias=bias_of(GATE_A), scale=0.5).then_inc(gate_read, 1)
                if not i0:
                    act.wait_ge(u_done, i)
                nc.scalar.activation(tmp[:, :], bank_of(0), ACT.Tanh, bias=bias_of(GATE_A), scale=0.5) \
                  .then_inc(gate_read, 1)
                high(t + 5, 0, 0)
                high(t + 5, 0, 1)
                for j in range(NT):
                    act.wait_ge(p_turned, i * NT + (j + 1))
                    nc.scalar.activation(pth[:, PT_AT[j]:PT_AT[j + 1]], ps[:, S0 + j, 0:PT_N[j]], ACT.Copy) \
                      .then_inc(pth_done, 1)
                tile_done(t + 4)
                if not i0:
                    act.wait_ge(conv_done, i)
                act.wait_ge(vec_const, 3)
                nc.scalar.activation(u[:, PAD:], bank_of(1), ACT.Identity, bias=bias_of(VAL), scale=0.5) \
                  .then_inc(val_read, 1)
                high(t + 6, 1, 0)
                high(t + 6, 1, 1)

            body(0, True)
            with nc.scalar.Fori(1, HEADS) as i:
                body(i, False)

            def gate_c(t, j, slot, par):
                tile_done(t)
                act.wait_ge(attn_done, HEADS)
                act.wait_ge(nowz_done, j + 1)
                if not isinstance(j, int) or j >= 4:
                    act.wait_ge(yc_done, j - 3)
                nc.scalar.activation(zbuf[:, slot, :], bank_of(par), ACT.Identity,
                                     bias=now_z[:, par:par + 1], scale=0.5).then_inc(z_read, 1)
                if isinstance(j, int) and j == 0:
                    act.wait_ge(u_done, HEADS)
                else:
                    act.wait_ge(z_done, j)
                nc.scalar.activation(tmp[:, :], bank_of(par), ACT.Tanh,
                                     bias=now_z[:, par:par + 1], scale=0.5).then_inc(z_read, 1)

            def finish_conv(j):
                act.wait_ge(norm_done, j + 1)
                if not isinstance(j, int) or j:
                    act.wait_ge(act_done, j)
                nc.scalar.activation(odd[:, :], sq[:, 0, :], ACT.Tanh, bias=now_n[:, 1:2], scale=now_n[:, 0:1]) \
                  .then_inc(aff_done, 1)
                nc.scalar.activation(sq[:, 1, :], sq[:, 0, :], ACT.Identity, bias=now_n[:, 1:2],
                                     scale=now_n[:, 0:1]).then_inc(aff_done, 1)

            t = T_GATE
            glu_gate(t - 1, HEADS - 1)
            high(t + 1, 0, 0)
            high(t + 1, 0, 1)
            gate_c(t, 0, 0, 1)
            high(t + 2, 1, 0)
            high(t + 2, 1, 1)
            gate_c(t + 1, 1, 1, 0)
            high(t + 3, 0, 0)
            high(t + 3, 0, 1)
            for j in range(HEADS):
                act.wait_ge(cent_done, j + 1)
                if j >= 3:
                    act.wait_ge(sqo_done if j % 2 == 0 else sqe_done, (j - 3) // 2 + 2)
                nc.scalar.activation(sq[:, j % 3, :], y[:, HEADS + j, :], ACT.Square).then_inc(sq_done, 1)
                if j in (1, 3):
                    high(t + 4, 1, j // 2)
                if j == 5:
                    gate_c(t + 2, 2, 2, 1)

            def root():
                act.wait_ge(rstd_vec, 1)
                nc.scalar.activation(odd[:, :], sq_odd[:, :], ACT.Ln).then_inc(rstd_act, 1)
                act.wait_ge(rstd_act, 1)
                nc.scalar.activation(rstd[:, :], odd[:, :], ACT.Exp, scale=-0.5).then_inc(rstd_act, 1)

            def gate_step(j, s):
                gate_c(j + (T_GATE - 1), j - 1, (s - 1) % 4, s % 2)
                high(j + (T_GATE + 1), s % 2, 0)
                if isinstance(j, int) and j == 4:
                    high(j + (T_GATE + 1), s % 2, 1)
                    root()
                    finish_conv(j - 4)
                else:
                    finish_conv(j - 4)
                    high(j + (T_GATE + 1), s % 2, 1)

            for j in range(4, 8):
                gate_step(j, j % 4)
            with nc.scalar.Fori(2, HEADS // 4) as b:
                for s in range(4):
                    gate_step(b * 4 + s, s)

            def y_tile(k):
                return y[:, ds(k, 1), :].rearrange("p a b -> p (a b)")

            def split_y(slot, src):
                nc.scalar.activation(yh[:, slot, :], src, ACT.Copy).then_inc(yh_done, 1)

            def out_pair(pair, m, s, nxt, conv_tile=None):
                t = pair + T_OUT
                high(t + 1, s, 0, lag=3)
                split_y(1, y_tile(m * 2 + 1))
                if conv_tile is not None:
                    finish_conv(conv_tile)
                high(t + 1, s, 1, lag=3)
                split_y(0, y_tile(nxt))

            act.wait_ge(attn_done, HEADS)
            split_y(0, y_tile(0))
            gate_c(T_OUT - 1, HEADS - 1, 3, 0)
            for m in range(4):
                out_pair(m, m, m % 2, 2 * m + 2, HEADS - 4 + m)
            with nc.scalar.Fori(2, OUT_PAIRS // 4) as b:
                for s in range(2):
                    out_pair(b * 2 + s, b * 2 + s, s, b * 4 + (2 * s + 2))
            act.wait_ge(yc_done, HEADS)
            with nc.scalar.Fori(OUT_PAIRS // 4, OUT_PAIRS // 2 - 1) as b:
                for s in range(2):
                    out_pair(b * 2 + s, b * 2 + s, s, b * 4 + (2 * s + 2))
            out_pair(OUT_PAIRS - 2, OUT_PAIRS - 2, 0, 2 * OUT_PAIRS - 2)
            out_pair(OUT_PAIRS - 1, OUT_PAIRS - 1, 1, 0)
            with nc.scalar.Fori(0, OUT_PAIRS // 2 - 3) as b:
                for s in range(2):
                    out_pair(b * 2 + (OUT_PAIRS + s), b * 2 + s, s, b * 4 + (2 * s + 2))
            out_pair(N_OUT - 6, OUT_PAIRS - 6, 0, PER_PASS - END - 2)
            act.wait_ge(half_done, 2 * T_OUT + E0 - 2)
            split_y(1, y_tile(PER_PASS - END - 1))
            for q in range(END):
                t, h = T_OUT + (E0 + q) // 2, q % 2
                act.wait_ge(raw_full[h], 16 * (t + 1))
                if q >= 4:
                    act.wait_ge(half_done, 2 * T_OUT + E0 - 1 + h)
                o = wh_last[:, q, :] if q < 4 else wh[:, (2 * T_OUT + q) % SLOTS, :]
                nc.scalar.activation(o, raw[:, h, :], ACT.Copy).then_inc(high_done, 1)
                nc.scalar.activation(end_y(yh, yh_last, yh_end, q), y_tile(PER_PASS - END + q), ACT.Copy) \
                  .then_inc(yh_done, 1)

            for n in range(NT):
                act.wait_ge(fin_vec, FIN * n + 4)
                nc.scalar.activation(std[:, :], var_eps[:, :], ACT.Sqrt).then_inc(fin_act, 1)

        @block.tensor
        def _(pe):
            def mm3(o, ah, al, bh, bl, start):
                nc.tensor.matmul(o, ah, bh, start=start, stop=False, skip_group_check=True)
                nc.tensor.matmul(o, ah, bl, start=False, stop=False, skip_group_check=True)
                return nc.tensor.matmul(o, al, bh, start=False, stop=True, skip_group_check=True)

            def half(t, par, h, beside=None):
                pe.wait_ge(low_done, 2 * t + (h + 1))
                for k in range(HALF):
                    if beside is not None:
                        beside(k)
                    a = slice(P * k, P * (k + 1))
                    last = mm3(ps[:, par, :], wh[:, 2 * par + h, a], wl[:, 2 * par + h, a],
                               xh[:, HALF * h + k, :], xl[:, HALF * h + k, :], h == 0 and k == 0)
                last.then_inc(half_done, 1)

            pe.wait_ge(const_done, 3)
            def turn_x(kt):
                if P * kt in X_CUTS:
                    pe.wait_ge(x_loaded[X_CUTS.index(P * kt)], 16)
                if kt >= 4:
                    pe.wait_ge(xl_done, kt - 3)
                for n in range(NT):
                    last = nc.tensor.transpose(ps[:, S0 + kt % 4, P * n:P * (n + 1)],
                                               x_rows[:, n, P * kt:P * (kt + 1)], ident[:, :])
                last.then_inc(xt_turned, 1)

            for kt in range(KT + 4):
                if kt < KT:
                    turn_x(kt)
                k = kt - 4
                if k >= 0:
                    if k % HALF == 0:
                        pe.wait_ge(f_pad, k // HALF + 1)
                        pe.wait_ge(low_done, k // HALF + 1)
                    if kt >= KT:
                        pe.wait_ge(xl_done, k + 1)
                    w = f_w[k // HALF][:, k % HALF, :]
                    nc.tensor.matmul(ps[0:LOW_AT + HEADS, 0, :], w[:, 0:LOW_AT + HEADS], xh[:, k, :],
                                     start=k == 0, stop=False, skip_group_check=True)
                    last = nc.tensor.matmul(ps[0:HEADS, 0, :], w[:, 0:HEADS], xl[:, k, :],
                                            start=False, stop=True, skip_group_check=True)
                    if k % HALF == HALF - 1:
                        last.then_inc(half_done, 1)
            pe.wait_ge(rows_loaded, 16 * 7)
            nc.tensor.transpose(ps[:, V_BANK, 0:7 * HEADS], rows[0:7 * HEADS, D:D + P], ident[0:7 * HEADS, 0:7 * HEADS])
            nc.tensor.transpose(ps[:, V_BANK, 128:128 + 3 * HEADS], rows[0:3 * HEADS, D + P:D + 2 * P],
                                ident[0:3 * HEADS, 0:3 * HEADS]).then_inc(cols_turned, 1)
            for c in range(HEADS):
                last = nc.tensor.transpose(ps[:, O_BANK, TAPS * c:TAPS * (c + 1)], rows[0:TAPS, P * c:P * (c + 1)],
                                           ident[0:TAPS, 0:TAPS])
            last.then_inc(cols_turned, 1)

            def body(i, i0):
                t = i * PER_HEAD + T_BODY
                if not i0:
                    pe.wait_ge(val_read, i)
                half(t, 1, 0)
                half(t, 1, 1)
                if i0:
                    pe.wait_ge(f_vec, 5)
                    for b in range(NT):
                        last = nc.tensor.transpose(ps[:, O_BANK, HEADS * b:HEADS * (b + 1)], fcum[:, P * b:P * (b + 1)],
                                                   ident[0:HEADS, 0:HEADS])
                    last.then_inc(cum_turned, 1)
                else:
                    pe.wait_ge(glu_tanh, i)
                half(t + 1, 0, 0)
                half(t + 1, 0, 1)
                pe.wait_ge(qk_low, i * 2 + 1)
                half(t + 2, 1, 0)
                pe.wait_ge(qk_low, i * 2 + 2)
                if not i0:
                    pe.wait_ge(ptl_done, i * NT)
                for b in range(NT):
                    o, m, c = ps[:, S0 + b, 0:P * (b + 1)], slice(P * b, P * (b + 1)), slice(0, P * (b + 1))
                    mm3(o, qh[:, m], ql[:, m], kh[:, c], kl[:, c], True).then_inc(scores_done, 1)
                half(t + 2, 1, 1)
                half(t + 3, 0, 0)
                pe.wait_ge(vt_done, i + 1)
                if not i0:
                    pe.wait_ge(vl_done, i)
                for b in range(NT):
                    last = nc.tensor.transpose(ps[:, V_BANK, P * b:P * (b + 1)], v_t[:, P * b:P * (b + 1)], ident[:, :])
                last.then_inc(v_turned, 1)
                half(t + 3, 0, 1)
                half(t + 4, 1, 0)
                pe.wait_ge(probs_done, i * NT + NT)
                for j in range(NT):
                    for b in range(j, NT):
                        last = nc.tensor.transpose(ps[:, S0 + j, P * (b - j):P * (b - j + 1)],
                                                   probs[:, PR_AT[b] + P * j:PR_AT[b] + P * (j + 1)], ident[:, :])
                    last.then_inc(p_turned, 1)
                half(t + 4, 1, 1)
                pe.wait_ge(gate_read, i * 2 + 2)
                half(t + 5, 0, 0)
                pe.wait_ge(ptl_done, i * NT + NT)
                pe.wait_ge(vl_done, i + 1)
                if not i0:
                    pe.wait_ge(attn_done, i)
                for j in range(NT):
                    a, c = slice(P * j, P * (j + 1)), slice(PT_AT[j], PT_AT[j + 1])
                    last = mm3(ps[:, O_BANK, P * j:SEQ], vh[:, a], vl[:, a], pth[:, c], ptl[:, c], j == 0)
                last.then_inc(pv_done, 1)
                half(t + 5, 0, 1)

            body(0, True)
            with nc.tensor.Fori(1, HEADS) as i:
                body(i, False)

            for j in range(4):
                if j == 0:
                    pe.wait_ge(val_read, HEADS)
                elif j == 1:
                    pe.wait_ge(glu_tanh, HEADS)
                else:
                    pe.wait_ge(z_read, 2 * j - 2)
                half(T_GATE + j, (j + 1) % 2, 0)
                half(T_GATE + j, (j + 1) % 2, 1)
                if j == 2:
                    pe.wait_ge(csum_done, HEADS)
                    pe.wait_ge(vl_done, HEADS)
                    nc.tensor.matmul(ps[:, V_BANK, :], mean_w[:, :], csum[:, :], start=True, stop=True) \
                      .then_inc(mean_done, 1)
            pe.wait_ge(z_read, 6)
            half(T_GATE + 4, 1, 0)

            def variance(k):
                if k != 2:
                    return
                pe.wait_ge(sqe_done, HEADS // 2 + 1)
                pe.wait_ge(sqo_done, HEADS // 2 + 1)
                pe.wait_ge(attn_done, HEADS)
                nc.tensor.matmul(ps[:, O_BANK, :], mean_w[:, :], csum[:, :], start=True, stop=False)
                nc.tensor.matmul(ps[:, O_BANK, :], mean_w[:, :], sq_odd[:, :], start=False, stop=True) \
                  .then_inc(var_done, 1)

            half(T_GATE + 4, 1, 1, variance)
            for j in range(5, 8):
                pe.wait_ge(z_read, 2 * j - 2)
                half(T_GATE + j, (j + 1) % 2, 0)
                half(T_GATE + j, (j + 1) % 2, 1)
            with nc.tensor.Fori(2, HEADS // 4) as b:
                for s in range(4):
                    pe.wait_ge(z_read, b * 8 + (2 * s - 2))
                    half(b * 4 + (T_GATE + s), (s + 1) % 2, 0)
                    half(b * 4 + (T_GATE + s), (s + 1) % 2, 1)

            def bank(n, g):
                return (2 * n + g + 2) % 8

            def ready(step):
                pe.wait_ge(low_done, step + (2 * T_OUT + 1))
                pe.wait_ge(yl_done, step + 1)

            def slot_of(q):
                return (2 * T_OUT + q) % SLOTS

            def step_mm(q, tokens=range(NT)):
                for n in tokens:
                    for g in range(2):
                        a, c = slice(P * n, P * (n + 1)), slice(SEQ * g, SEQ * (g + 1))
                        last = mm3(ps[:, bank(n, g), :], yh[:, q % 2, a], yl[:, q % 2, a],
                                   wh[:, slot_of(q), c], wl[:, slot_of(q), c], False)
                return last

            def end_mm(q, n, g):
                a, c = slice(P * n, P * (n + 1)), slice(SEQ * g, SEQ * (g + 1))
                if q < 4:
                    high_w, low_w = wh_last[:, q, c], wl_last[:, q, c]
                else:
                    high_w, low_w = (w[:, slot_of(q), c] for w in (wh, wl))
                return mm3(ps[:, bank(n, g), :], end_y(yh, yh_last, yh_end, q)[:, a], end_y(yl, yl_last, yl_end, q)[:, a],
                           high_w, low_w, False)

            for p in range(2):
                at = p * PER_PASS
                ready(at)
                if p == 0:
                    pe.wait_ge(rstd_vec, 2)
                    pe.wait_ge(cent_done, HEADS)
                    pe.wait_ge(ptl_done, HEADS * NT)
                for n in range(NT):
                    for g in range(2):
                        if p == 0 and bank(n, g) < 2:
                            pe.wait_ge(z_read, 2 * HEADS)
                        if p == 1:
                            pe.wait_ge(evac_done, 2 * n + g + 1)
                        a, c = slice(P * n, P * (n + 1)), slice(SEQ * g, SEQ * (g + 1))
                        last = mm3(ps[:, bank(n, g), :], yh[:, 0, a], yl[:, 0, a],
                                   wh[:, slot_of(0), c], wl[:, slot_of(0), c], True)
                last.then_inc(half_done, 1)
                for q in range(1, 4):
                    ready(at + q)
                    step_mm(q).then_inc(half_done, 1)
                with nc.tensor.Fori(1, PER_PASS // 4 - (1 if p == 0 else 2)) as b:
                    for q in range(4):
                        ready(b * 4 + (at + q))
                        step_mm(q).then_inc(half_done, 1)
                if p == 0:
                    for q in range(3):
                        ready(at + PER_PASS - 4 + q)
                        step_mm(q).then_inc(half_done, 1)
                    ready(at + PER_PASS - 1)
                    for n in range(NT):
                        step_mm(3, [n]).then_inc(sum_done if n < NT - 1 else half_done, 1)
            for n, qs in ((0, range(4)), (1, range(4)), (0, range(4, END)), (1, range(4, END)),
                          (2, range(END)), (3, range(END))):
                for g in range(2):
                    for q in qs:
                        if n == 0 and g == 0:
                            ready(E0 + q)
                        last = end_mm(q, n, g)
                    if qs[-1] == END - 1:
                        last.then_inc(half_done, 1)

        @block.vector
        def _(dve):
            vec = nc.vector

            def low(t, par, h):
                dve.wait_ge(high_done, 2 * t + (h + 1))
                vec.tensor_tensor(wl[:, 2 * par + h, :], raw[:, h, :], wh[:, 2 * par + h, :], ALU.subtract) \
                   .then_inc(low_done, 1)

            def col(table, kind, i):
                return table[:, ds(kind * HEADS + i, 1)]

            def y_tile(k):
                return y[:, ds(k, 1), :].rearrange("p a b -> p (a b)")

            vec.memset(mean_w[:, :], 1.0 / D).then_inc(vec_const, 1)
            vec.memset(one[:, :], 1.0).then_inc(vec_const, 1)
            vec.memset(u[:, 0:PAD], 0.0).then_inc(vec_const, 1)
            for h in range(2):
                vec.memset(f_w[h][:, :, HEADS:LOW_AT].bitcast(F32), 0.0).then_inc(f_pad, 1)
            vec.memset(csum[:, :], 0.0).then_inc(vec_const, 1)

            def x_low(kt):
                dve.wait_ge(xh_done, kt + 1)
                vec.tensor_tensor(xl[:, kt, :], ps[:, S0 + kt % 4, :], xh[:, kt, :], ALU.subtract).then_inc(xl_done, 1)

            for kt in range(KT):
                x_low(kt)
                if kt in (1, 2):
                    h = kt - 1
                    dve.wait_ge(high_done, h + 1)
                    vec.tensor_tensor(f_w[h][:, :, LOW_AT:LOW_AT + HEADS], f_raw[h], f_w[h][:, :, 0:HEADS],
                                      ALU.subtract).then_inc(low_done, 1)
            low(1, 1, 0)
            low(1, 1, 1)
            dve.wait_ge(cols_done, 5)

            def conv(i, n0, n1):
                for w in range(n0, n1):
                    o = odd[:, :] if w % 2 else y_tile(HEADS + i)
                    if w > 1:
                        dve.wait_ge(tap_done, i * TAPS + (w - 1))
                    tap = taps[:, ds(i, 1), w]
                    if w == 0:
                        ins = vec.tensor_scalar(o, u[:, 0:SEQ], tap, col(cn, B_DW, i), ALU.mult, ALU.add)
                    elif w == 1:
                        if not isinstance(i, int) or i:
                            dve.wait_ge(conv_done, i)
                        ins = vec.tensor_scalar(o, u[:, w:w + SEQ], tap, None, ALU.mult)
                    else:
                        ins = vec.scalar_tensor_tensor(out=o, in0=u[:, w:w + SEQ], scalar=tap, in1=o,
                                                       op0=ALU.mult, op1=ALU.add)
                    ins.then_inc(tap_done, 1)

            def conv_end(i):
                dve.wait_ge(tap_done, i * TAPS + TAPS)
                vec.tensor_tensor(y_tile(HEADS + i), y_tile(HEADS + i), odd[:, :], ALU.add).then_inc(conv_done, 1)

            def glu(i):
                dve.wait_ge(val_read, i + 1)
                dve.wait_ge(glu_tanh, i + 1)
                vec.scalar_tensor_tensor(out=u[:, PAD:], in0=tmp[:, :], scalar=1.0, in1=u[:, PAD:],
                                         op0=ALU.add, op1=ALU.mult).then_inc(u_done, 1)
                dve.wait_ge(u_done, i + 1)

            def body(i, i0):
                t = i * PER_HEAD + T_BODY
                at = [sum(BODY_TAPS[:s]) for s in range(PER_HEAD + 1)]

                def taps_of(s, part):
                    if i0:
                        return
                    mid = (at[s] + at[s + 1] + 1) // 2
                    lo, hi = (at[s], mid) if part == 0 else (mid, at[s + 1])
                    conv(i - 1, lo, min(hi, TAPS))
                    if lo < TAPS <= hi:
                        conv_end(i - 1)

                if i0:
                    forget()
                else:
                    glu(i - 1)
                for kind, (at_col, halved) in NOW.items():
                    ins = vec.tensor_copy(now[:, at_col:at_col + 1], col(hcols if halved else cols, kind, i))
                ins.then_inc(now_done, 1)
                low(t + 1, 0, 0)
                taps_of(0, 0)
                low(t + 1, 0, 1)
                taps_of(0, 1)
                dve.wait_ge(qk_high, i * 2 + 1)
                vec.scalar_tensor_tensor(out=ql, in0=ps[:, 1, :], scalar=col(cols, Q, i), in1=qh,
                                         op0=ALU.add, op1=ALU.subtract).then_inc(qk_low, 1)
                if i0:
                    dve.wait_ge(cum_turned, 1)
                    vec.tensor_copy(cum_t[:, :, :].rearrange("p h b -> p b h"),
                                    ps[:, O_BANK, 0:NT * HEADS].rearrange("p (b h) -> p b h", b=NT)).then_inc(cum_t_done, 1)
                    dve.wait_ge(cum_t_done, 1)
                else:
                    dve.wait_ge(bias_summed, i * NT)
                vec.tensor_copy(now_cum[:, :], cum_t[:, ds(i, 1), :].rearrange("p a b -> p (a b)")).then_inc(now_cum_done, 1)
                low(t + 2, 1, 0)
                taps_of(1, 0)
                low(t + 2, 1, 1)
                taps_of(1, 1)
                dve.wait_ge(qk_high, i * 2 + 2)
                vec.scalar_tensor_tensor(out=kl, in0=ps[:, 0, :], scalar=col(cols, K, i), in1=kh,
                                         op0=ALU.add, op1=ALU.subtract).then_inc(qk_low, 1)
                low(t + 3, 0, 0)
                taps_of(2, 0)
                low(t + 3, 0, 1)
                if not i0:
                    dve.wait_ge(negmax_done, i)
                dve.wait_ge(bias_done, i * NT + NT)
                for b in range(NT):
                    dve.wait_ge(scores_done, i * NT + (b + 1))
                    vec.memset(waited[:, b:b + 1], 0.0).then_inc(max_done, 1)
                    o = probs[:, PR_AT[b]:PR_AT[b + 1]]
                    vec.tensor_tensor_reduce(o, ps[:, S0 + b, 0:P * (b + 1)], o, 1.0, 4.0 * MASKED, ALU.add, ALU.max,
                                             row_max[:, b:b + 1]).then_inc(max_done, 1)
                dve.wait_ge(max_done, i * (2 * NT) + 2 * NT)
                vec.tensor_scalar(neg_max[:, :], row_max[:, :], -SCALE, None, ALU.mult).then_inc(negmax_done, 1)
                taps_of(2, 1)
                dve.wait_ge(exp_done, i * NT + NT)
                vec.reciprocal(row_inv[:, :], row_sum[:, :]).then_inc(inv_done, 1)
                dve.wait_ge(inv_done, i + 1)
                for b in range(NT):
                    pr = probs[:, PR_AT[b]:PR_AT[b + 1]]
                    vec.tensor_scalar(pr, pr, row_inv[:, b:b + 1], None, ALU.mult).then_inc(probs_done, 1)
                low(t + 4, 1, 0)
                taps_of(3, 0)
                low(t + 4, 1, 1)
                dve.wait_ge(vh_done, i + 1)
                vec.tensor_tensor(vl[:, :], ps[:, V_BANK, :], vh[:, :], ALU.subtract).then_inc(vl_done, 1)
                taps_of(3, 1)
                dve.wait_ge(gate_read, i * 2 + 2)
                vec.scalar_tensor_tensor(out=y_tile(i), in0=tmp[:, :], scalar=1.0, in1=v_t[:, :],
                                         op0=ALU.add, op1=ALU.mult).then_inc(gate_done, 1)
                low(t + 5, 0, 0)
                taps_of(4, 0)
                low(t + 5, 0, 1)
                for j in range(NT):
                    dve.wait_ge(pth_done, i * NT + (j + 1))
                    c = slice(PT_AT[j], PT_AT[j + 1])
                    vec.tensor_tensor(ptl[:, c], ps[:, S0 + j, 0:PT_N[j]], pth[:, c], ALU.subtract).then_inc(ptl_done, 1)
                taps_of(4, 1)
                low(t + 6, 1, 0)
                low(t + 6, 1, 1)
                dve.wait_ge(pv_done, i + 1)
                dve.wait_ge(gate_done, i + 1)
                vec.tensor_tensor(y_tile(i), ps[:, O_BANK, :], y_tile(i), ALU.mult).then_inc(attn_done, 1)

            def forget():
                dve.wait_ge(f_act, 1)
                dve.wait_ge(rows_loaded, 16 * 7)
                vec.scalar_tensor_tensor(out=fz, in0=ps[0:HEADS, 0, :], scalar=fbias[:, :], in1=f_low,
                                         op0=ALU.add, op1=ALU.add).then_inc(f_vec, 1)
                dve.wait_ge(f_act, 4)
                vec.scalar_tensor_tensor(out=fm, in0=fz, scalar=0.0, in1=fa, op0=ALU.min, op1=ALU.subtract) \
                   .then_inc(f_vec, 1)
                dve.wait_ge(f_vec, 2)
                vec.tensor_tensor_scan(fcum, one_row, fm, 0.0, ALU.mult, ALU.add).then_inc(f_vec, 1)
                dve.wait_ge(f_vec, 3)
                vec.tensor_scalar(neg_cum, fcum, -1.0 / SCALE, None, ALU.mult).then_inc(f_vec, 1)
                vec.tensor_scalar(fcum, fcum, 1.0 / SCALE, None, ALU.mult).then_inc(f_vec, 1)
            one_row = odd[0:HEADS, :]
            vec.memset(one_row, 1.0).then_inc(vec_const, 1)
            dve.wait_ge(vec_const, 5)

            body(0, True)
            with vec.Fori(1, HEADS) as i:
                body(i, False)

            def bias_z(j, par):
                if not isinstance(j, int) or j >= 2:
                    dve.wait_ge(z_read, j * 2 - 2)
                vec.tensor_copy(now_z[:, par:par + 1], col(hcols, GATE_C, j)).then_inc(nowz_done, 1)

            def gate(j, slot):
                dve.wait_ge(z_read, j * 2 + 2)
                vec.scalar_tensor_tensor(out=zbuf[:, slot, :], in0=tmp[:, :], scalar=1.0, in1=zbuf[:, slot, :],
                                         op0=ALU.add, op1=ALU.mult).then_inc(z_done, 1)

            def normed(j):
                dve.wait_ge(rstd_vec, 6)
                if not isinstance(j, int) or j:
                    dve.wait_ge(aff_done, j * 2)
                vec.tensor_copy(now_n[:, 0:1], hcn[:, ds(G_CN * HEADS + j, 1)]).then_inc(nown_done, 1)
                vec.tensor_copy(now_n[:, 1:2], hcn[:, ds(B_CN * HEADS + j, 1)]).then_inc(nown_done, 1)
                dve.wait_ge(nown_done, j * 2 + 2)
                vec.tensor_tensor(sq[:, 0, :], y_tile(HEADS + j), rstd[:, :], ALU.mult).then_inc(norm_done, 1)

            def gated(j, slot):
                dve.wait_ge(aff_done, j * 2 + 2)
                vec.scalar_tensor_tensor(out=y_tile(HEADS + j), in0=odd[:, :], scalar=1.0, in1=sq[:, 1, :],
                                         op0=ALU.add, op1=ALU.mult).then_inc(act_done, 1)
                dve.wait_ge(act_done, j + 1)
                dve.wait_ge(z_done, j + 1)
                vec.tensor_tensor(y_tile(HEADS + j), y_tile(HEADS + j), zbuf[:, slot, :], ALU.mult).then_inc(yc_done, 1)

            t, c = T_GATE, HEADS - 1
            for j in range(2):
                bias_z(j, (j + 1) % 2)
            glu(c)
            low(t + 1, 0, 0)
            conv(c, 0, 6)
            low(t + 1, 0, 1)
            conv(c, 6, 16)
            gate(0, 0)
            bias_z(2, 1)
            low(t + 2, 1, 0)
            conv(c, 16, 24)
            low(t + 2, 1, 1)
            conv(c, 24, TAPS)
            conv_end(c)
            gate(1, 1)
            bias_z(3, 0)
            low(t + 3, 0, 0)
            low(t + 3, 0, 1)
            vec.memset(sq_odd[:, :], 0.0).then_inc(sqo_done, 1)

            def center(j):
                vec.tensor_tensor(y_tile(HEADS + j), y_tile(HEADS + j), ps[:, V_BANK, :], ALU.subtract).then_inc(cent_done, 1)

            def add_square(j):
                dve.wait_ge(sq_done, j + 1)
                dve.wait_ge(sqo_done, (j - 1) // 2 + 1)
                vec.tensor_tensor(sq_odd[:, :], sq_odd[:, :], sq[:, j % 3, :], ALU.add).then_inc(sqo_done, 1)

            dve.wait_ge(mean_done, 1)
            for j in range(HEADS):
                center(j)
                if j >= 4 and j % 2 == 0:
                    add_square(j - 3)
                if j in (5, 7):
                    low(t + 4, 1, (j - 5) // 2)
                if j == 11:
                    gate(2, 2)
            add_square(HEADS - 3)
            add_square(HEADS - 1)

            def root():
                dve.wait_ge(var_done, 1)
                vec.tensor_scalar(sq_odd[:, :], ps[:, O_BANK, :], LN_EPS, None, ALU.add).then_inc(rstd_vec, 1)
                dve.wait_ge(rstd_act, 2)
                vec.tensor_tensor(odd[:, :], rstd[:, :], rstd[:, :], ALU.mult).then_inc(rstd_vec, 1)
                dve.wait_ge(rstd_vec, 2)
                vec.tensor_tensor(odd[:, :], odd[:, :], sq_odd[:, :], ALU.mult).then_inc(rstd_vec, 1)
                dve.wait_ge(rstd_vec, 3)
                vec.tensor_scalar(odd[:, :], odd[:, :], -0.5, 1.5, ALU.mult, ALU.add).then_inc(rstd_vec, 1)
                dve.wait_ge(rstd_vec, 4)
                vec.tensor_tensor(rstd[:, :], rstd[:, :], odd[:, :], ALU.mult).then_inc(rstd_vec, 2)

            def gate_step(j, s):
                gate(j - 1, (s - 1) % 4)
                bias_z(j, (s + 1) % 2)
                low(j + (T_GATE + 1), s % 2, 0)
                if isinstance(j, int) and j == 4:
                    low(j + (T_GATE + 1), s % 2, 1)
                    root()
                    normed(j - 4)
                else:
                    normed(j - 4)
                    low(j + (T_GATE + 1), s % 2, 1)
                gated(j - 4, s)

            for j in range(4, 8):
                gate_step(j, j % 4)
            with vec.Fori(2, HEADS // 4) as b:
                for s in range(4):
                    gate_step(b * 4 + s, s)

            def split_y(n, slot, src):
                dve.wait_ge(yh_done, n + 1)
                vec.tensor_tensor(yl[:, slot, :], src, yh[:, slot, :], ALU.subtract).then_inc(yl_done, 1)

            def out_pair(pair, m, s, nxt, conv_tile=None):
                t = pair + T_OUT
                if conv_tile is not None:
                    normed(conv_tile)
                low(t + 1, s, 0)
                split_y(pair * 2 + 1, 1, y_tile(m * 2 + 1))
                if conv_tile is not None:
                    gated(conv_tile, conv_tile % 4)
                low(t + 1, s, 1)
                split_y(pair * 2 + 2, 0, y_tile(nxt))

            split_y(0, 0, y_tile(0))
            gate(HEADS - 1, 3)
            for m in range(4):
                out_pair(m, m, m % 2, 2 * m + 2, HEADS - 4 + m)
            with vec.Fori(2, OUT_PAIRS // 2 - 1) as b:
                for s in range(2):
                    out_pair(b * 2 + s, b * 2 + s, s, b * 4 + (2 * s + 2))
            out_pair(OUT_PAIRS - 2, OUT_PAIRS - 2, 0, 2 * OUT_PAIRS - 2)
            out_pair(OUT_PAIRS - 1, OUT_PAIRS - 1, 1, 0)

            def add_result(p, n, before=None):
                for g in range(2):
                    if before is not None:
                        dve.wait_ge(half_done, before + g + 1)
                    r = res[:, n, 1024 * p + SEQ * g:1024 * p + SEQ * (g + 1)]
                    vec.tensor_tensor(r, ps[:, (2 * n + g + 2) % 8, :], r, ALU.add).then_inc(evac_done, 1)

            def row_stats(p, n):
                dve.wait_ge(evac_done, 8 * p + 2 * n + 2)
                for g in range(2 * p, 2 * p + 2):
                    ins = vec.bn_stats(stats[:, n, g, :], res[:, n, SEQ * g:SEQ * (g + 1)])
                return ins

            dve.wait_ge(res_ready, NT)
            for n in range(NT):
                if n < NT - 1:
                    dve.wait_ge(sum_done, n + 1)
                else:
                    dve.wait_ge(half_done, 2 * T_OUT + 2 * OUT_PAIRS)
                add_result(0, n)
            for m in range(4):
                out_pair(OUT_PAIRS + m, m, m % 2, 2 * m + 2)
                row_stats(0, m).then_inc(stats_done, 1)
            with vec.Fori(2, OUT_PAIRS // 2 - 3) as b:
                for s in range(2):
                    out_pair(b * 2 + (OUT_PAIRS + s), b * 2 + s, s, b * 4 + (2 * s + 2))
            out_pair(N_OUT - 6, OUT_PAIRS - 6, 0, PER_PASS - END - 2)
            split_y(E0 - 1, 1, y_tile(PER_PASS - END - 1))
            for q in range(END):
                dve.wait_ge(high_done, 2 * T_OUT + E0 + q + 1)
                if q < 4:
                    high_w, low_w = wh_last[:, q, :], wl_last[:, q, :]
                else:
                    high_w, low_w = (w[:, (2 * T_OUT + q) % SLOTS, :] for w in (wh, wl))
                vec.tensor_tensor(low_w, raw[:, q % 2, :], high_w, ALU.subtract).then_inc(low_done, 1)
                dve.wait_ge(yh_done, E0 + q + 1)
                vec.tensor_tensor(end_y(yl, yl_last, yl_end, q), y_tile(PER_PASS - END + q),
                                  end_y(yh, yh_last, yh_end, q), ALU.subtract).then_inc(yl_done, 1)

            dve.wait_ge(bcast_loaded, 48)
            dve.wait_ge(stats_done, NT)
            for n in range(NT):
                base = FIN * n
                add_result(1, n, 2 * T_OUT + E0 + 2 * n)
                row_stats(1, n).then_inc(fin_vec, 1)
                dve.wait_ge(fin_vec, base + 1)
                if n:
                    dve.wait_ge(row_done, 2 * n)
                vec.bn_aggr(mv[:, :], stats[:, n, :, :].rearrange("p a b -> p (a b)")).then_inc(fin_vec, 2)
                dve.wait_ge(fin_vec, base + 3)
                vec.tensor_scalar(var_eps[:, :], mv[:, 1:2], LN_EPS, None, ALU.add).then_inc(fin_vec, 1)
                for h in range(2):
                    r, c = res[:, n, 1024 * h:1024 * (h + 1)], slice(1024 * h, 1024 * (h + 1))
                    vec.scalar_tensor_tensor(out=r, in0=r, scalar=mv[:, 0:1], in1=gpost_b[:, c],
                                             op0=ALU.subtract, op1=ALU.mult).then_inc(scaled_done, 1)
                dve.wait_ge(fin_act, n + 1)
                vec.reciprocal(rs[:, :], std[:, :]).then_inc(fin_vec, 1)
                dve.wait_ge(fin_vec, base + 5)
                vec.scalar_tensor_tensor(out=newton[:, :], in0=rs[:, :], scalar=var_eps[:, :], in1=rs[:, :],
                                         op0=ALU.mult, op1=ALU.mult).then_inc(fin_vec, 1)
                dve.wait_ge(fin_vec, base + 6)
                vec.tensor_scalar(newton[:, :], newton[:, :], -0.5, 1.5, ALU.mult, ALU.add).then_inc(fin_vec, 1)
                dve.wait_ge(fin_vec, base + 7)
                vec.tensor_tensor(rs[:, :], rs[:, :], newton[:, :], ALU.mult).then_inc(fin_vec, 1)
                dve.wait_ge(fin_vec, base + 8)
                dve.wait_ge(scaled_done, 2 * n + 2)
                for h in range(2):
                    r, c = res[:, n, 1024 * h:1024 * (h + 1)], slice(1024 * h, 1024 * (h + 1))
                    vec.scalar_tensor_tensor(out=r, in0=r, scalar=rs[:, :], in1=bpost_b[:, c],
                                             op0=ALU.mult, op1=ALU.add).then_inc(row_done, 1)


_INS = ["x", "w_in", "b_in", "w_dw", "b_dw", "g_conv_norm", "b_conv_norm", "w_out", "b_out", "g_post", "b_post"]


def kernel(**inputs):
    import numpy as np
    import concourse.bacc as bacc
    from concourse.bass_utils import run_bass_kernel_spmd

    nc = bacc.Bacc("TRN2", target_bir_lowering=False, num_devices=1)
    arrays, args = {}, []
    for name in _INS:
        a = np.ascontiguousarray(inputs[name])
        arrays[f"in_{name}_dram"] = a
        args.append(nc.dram_tensor(f"in_{name}_dram", a.shape, mybir.dt.from_np(a.dtype), kind="ExternalInput").ap())
    out = nc.dram_tensor("out_0_dram", (1, SEQ, D), F32, kind="ExternalOutput").ap()
    scratch = nc.dram_tensor("forget_sums_dram", (HEADS, SEQ), F32).ap()
    build(nc, *args, out, scratch)
    r = run_bass_kernel_spmd(nc, [arrays], core_ids=[0])
    return r.results[0]["out_0_dram"]
```
